# Optimizing a Trainium2 kernel written in Bass

```python
import jax, jax.numpy as jnp
from jax import lax
import numpy as np

D_MODEL = 2048
BATCH = 1
SEQ = 256
DEPTH = 2

GRID_W = 64
N_MIXERS = 2
N_SSM_LAYERS = (DEPTH + N_MIXERS - 1) // N_MIXERS
N_NA_LAYERS = DEPTH // N_MIXERS
EXPAND = 2
SSM_D_INNER = EXPAND * D_MODEL
SSM_HEAD_DIM = 64
SSM_HEADS = SSM_D_INNER // SSM_HEAD_DIM
SSM_GROUPS = 8
SSM_STATE = 128
SSM_CONV_W = 7
SSM_CHUNK = 128
SSM_CONV_DIM = SSM_D_INNER + 2 * SSM_GROUPS * SSM_STATE
SSM_IN_DIM = SSM_D_INNER + SSM_CONV_DIM + 2 * SSM_HEADS
NA_D_INNER = EXPAND * D_MODEL
NA_HEAD_DIM = 128
NA_HEADS = NA_D_INNER // NA_HEAD_DIM
NA_WIN_H = 8
NA_WIN_W = 16
NA_IN_DIM = 4 * NA_D_INNER
NORM_EPS = 1e-5
DT_MIN = 1e-3
DT_MAX = 1e-1

kernel_name = "bidir_ssd_natten_hybrid"

def rmsnorm(x, w):
    xf = x.astype(jnp.float32)
    y = xf * lax.rsqrt(jnp.mean(xf * xf, axis=-1, keepdims=True) + NORM_EPS)
    return (y * w.astype(jnp.float32)).astype(x.dtype)

def centred_depthwise_conv(u, w, b):
    c = u.shape[-1]
    pad = SSM_CONV_W // 2
    out = lax.conv_general_dilated(
        u, w[:, None, :].astype(u.dtype), window_strides=(1,), padding=[(pad, pad)],
        dimension_numbers=('NWC', 'WIO', 'NWC'), feature_group_count=c)
    return out + b.astype(u.dtype)

def ssd_scan(x, dt, A, B, C):
    b, l, h, p = x.shape
    g, n = B.shape[2], B.shape[3]
    r = h // g
    cl = SSM_CHUNK
    nc = l // cl
    f32 = jnp.float32
    xdt = (x.astype(f32) * dt[..., None]).reshape(b, nc, cl, g, r, p)
    a_cum = jnp.cumsum((dt * A).reshape(b, nc, cl, g, r), axis=2)
    Bc = B.astype(f32).reshape(b, nc, cl, g, n)
    Cc = C.astype(f32).reshape(b, nc, cl, g, n)
    mask = jnp.tril(jnp.ones((cl, cl), dtype=bool))[:, :, None, None]
    seg = a_cum[:, :, :, None] - a_cum[:, :, None, :]
    decay = jnp.exp(jnp.where(mask, seg, -jnp.inf))
    cb = jnp.einsum('bclgn,bcsgn->bclsg', Cc, Bc)
    y_diag = jnp.einsum('bclsgr,bcsgrp->bclgrp', cb[..., None] * decay, xdt)
    decay_to_end = jnp.exp(a_cum[:, :, -1:] - a_cum)
    states = jnp.einsum('bcsgn,bcsgrp->bcgrpn', Bc, decay_to_end[..., None] * xdt)
    chunk_decay = jnp.exp(a_cum[:, :, -1])

    def step(carry, inp):
        st, dec = inp
        return carry * dec[..., None, None] + st, carry

    init = jnp.zeros((b, g, r, p, n), f32)
    _, prev = lax.scan(step, init, (jnp.moveaxis(states, 1, 0), jnp.moveaxis(chunk_decay, 1, 0)))
    prev = jnp.moveaxis(prev, 0, 1)
    y_off = jnp.einsum('bclgn,bcgrpn->bclgrp', Cc, prev) * jnp.exp(a_cum)[..., None]
    return (y_diag + y_off).reshape(b, l, h, p)

def mamba2_bidir_mixer(u, w_in, conv_w, conv_b, dt_bias, A_log, D, norm_w, w_out):
    b, l, _ = u.shape
    zxbcdt = u @ w_in
    z = zxbcdt[..., :SSM_D_INNER]
    xbc = zxbcdt[..., SSM_D_INNER:SSM_D_INNER + SSM_CONV_DIM]
    dt_raw = zxbcdt[..., SSM_D_INNER + SSM_CONV_DIM:].reshape(b, l, 2, SSM_HEADS)
    xbc = jax.nn.silu(centred_depthwise_conv(xbc, conv_w, conv_b))
    gn = SSM_GROUPS * SSM_STATE
    xs = xbc[..., :SSM_D_INNER].reshape(b, l, SSM_HEADS, SSM_HEAD_DIM)
    Bm = xbc[..., SSM_D_INNER:SSM_D_INNER + gn].reshape(b, l, SSM_GROUPS, SSM_STATE)
    Cm = xbc[..., SSM_D_INNER + gn:].reshape(b, l, SSM_GROUPS, SSM_STATE)
    dt = jax.nn.softplus(dt_raw.astype(jnp.float32) + dt_bias.astype(jnp.float32))
    A = -jnp.exp(A_log.astype(jnp.float32))
    y_fwd = ssd_scan(xs, dt[:, :, 0], A[0], Bm, Cm)
    flip = lambda t: jnp.flip(t, axis=1)
    y_bwd = flip(ssd_scan(flip(xs), flip(dt[:, :, 1]), A[1], flip(Bm), flip(Cm)))
    y = y_fwd + y_bwd + D.astype(jnp.float32)[:, None] * xs.astype(jnp.float32)
    y = y.reshape(b, l, SSM_D_INNER).astype(u.dtype)
    y = rmsnorm(y * jax.nn.silu(z), norm_w)
    return y @ w_out

def neighbourhood_attention(q, k, v, rpb):
    b, l, h, dh = q.shape
    rows = l // GRID_W
    kh = min(NA_WIN_H, rows)
    kw = NA_WIN_W
    scale = dh ** -0.5
    qg = q.reshape(b, rows, GRID_W, h, dh)
    kg = k.reshape(b, rows, GRID_W, h, dh)
    vg = v.reshape(b, rows, GRID_W, h, dh)
    row_start = jnp.clip(jnp.arange(rows) - kh // 2, 0, rows - kh)
    cols = jnp.arange(GRID_W)
    col_start = jnp.clip(cols - kw // 2, 0, GRID_W - kw)
    col_idx = col_start[:, None] + jnp.arange(kw)[None, :]
    col_off = col_idx - cols[:, None] + (NA_WIN_W - 1)

    def one_row(args):
        r, q_row = args
        rs = row_start[r]
        k_band = lax.dynamic_slice_in_dim(kg, rs, kh, axis=1)
        v_band = lax.dynamic_slice_in_dim(vg, rs, kh, axis=1)
        k_win = k_band[:, :, col_idx]
        v_win = v_band[:, :, col_idx]
        s = jnp.einsum('bqhd,biqjhd->bhqij', q_row, k_win).astype(jnp.float32) * scale
        row_off = rs + jnp.arange(kh) - r + (NA_WIN_H - 1)
        bias = rpb[:, row_off][:, :, col_off]
        s = s + jnp.transpose(bias, (0, 2, 1, 3)).astype(jnp.float32)[None]
        pr = jax.nn.softmax(s.reshape(b, h, GRID_W, kh * kw), axis=-1)
        pr = pr.reshape(b, h, GRID_W, kh, kw).astype(v.dtype)
        return jnp.einsum('bhqij,biqjhd->bqhd', pr, v_win)

    out = lax.map(one_row, (jnp.arange(rows), jnp.moveaxis(qg, 1, 0)))
    return jnp.moveaxis(out, 0, 1).reshape(b, l, h, dh)

def natten_mixer(u, w_in, rpb, w_out):
    b, l, _ = u.shape
    qkvz = u @ w_in
    q, k, v, z = jnp.split(qkvz, 4, axis=-1)
    shp = (b, l, NA_HEADS, NA_HEAD_DIM)
    o = neighbourhood_attention(q.reshape(shp), k.reshape(shp), v.reshape(shp), rpb)
    o = o.reshape(b, l, NA_D_INNER) * jax.nn.silu(z)
    return o @ w_out

def setup_inputs(seed: int = 0) -> dict:
    key = jax.random.key(seed)
    ks = jax.random.split(key, 16)
    f32 = jnp.float32
    NS, NN = N_SSM_LAYERS, N_NA_LAYERS
    x = jax.random.normal(ks[0], (BATCH, SEQ, D_MODEL), f32)
    norm_w = 1.0 + 0.02 * jax.random.normal(ks[1], (DEPTH, D_MODEL), f32)
    ssm_w_in = jax.random.normal(ks[2], (NS, D_MODEL, SSM_IN_DIM), f32) * D_MODEL ** -0.5
    ssm_conv_w = jax.random.normal(ks[3], (NS, SSM_CONV_W, SSM_CONV_DIM), f32) * SSM_CONV_W ** -0.5
    ssm_conv_b = 0.02 * jax.random.normal(ks[4], (NS, SSM_CONV_DIM), f32)
    dt0 = jnp.exp(jax.random.uniform(ks[5], (NS, 2, SSM_HEADS), f32,
                                     np.log(DT_MIN), np.log(DT_MAX)))
    ssm_dt_bias = dt0 + jnp.log(-jnp.expm1(-dt0))
    ssm_A_log = jnp.log(jax.random.uniform(ks[6], (NS, 2, SSM_HEADS), f32, 1.0, 16.0))
    ssm_D = 1.0 + 0.1 * jax.random.normal(ks[7], (NS, SSM_HEADS), f32)
    ssm_norm_w = 1.0 + 0.02 * jax.random.normal(ks[8], (NS, SSM_D_INNER), f32)
    ssm_w_out = jax.random.normal(ks[9], (NS, SSM_D_INNER, D_MODEL), f32) * SSM_D_INNER ** -0.5
    na_w_in = jax.random.normal(ks[10], (NN, D_MODEL, NA_IN_DIM), f32) * D_MODEL ** -0.5
    na_rpb = 0.1 * jax.random.normal(ks[11], (NN, NA_HEADS, 2 * NA_WIN_H - 1, 2 * NA_WIN_W - 1), f32)
    na_w_out = jax.random.normal(ks[12], (NN, NA_D_INNER, D_MODEL), f32) * NA_D_INNER ** -0.5
    final_norm_w = 1.0 + 0.02 * jax.random.normal(ks[13], (D_MODEL,), f32)
    return {"x": x, "norm_w": norm_w, "ssm_w_in": ssm_w_in, "ssm_conv_w": ssm_conv_w,
            "ssm_conv_b": ssm_conv_b, "ssm_dt_bias": ssm_dt_bias, "ssm_A_log": ssm_A_log,
            "ssm_D": ssm_D, "ssm_norm_w": ssm_norm_w, "ssm_w_out": ssm_w_out,
            "na_w_in": na_w_in, "na_rpb": na_rpb, "na_w_out": na_w_out,
            "final_norm_w": final_norm_w}

def reference(x, norm_w, ssm_w_in, ssm_conv_w, ssm_conv_b, ssm_dt_bias, ssm_A_log, ssm_D,
              ssm_norm_w, ssm_w_out, na_w_in, na_rpb, na_w_out, final_norm_w):
    h = x
    for i in range(DEPTH):
        u = rmsnorm(h, norm_w[i])
        j = i // N_MIXERS
        if i % N_MIXERS == 0:
            h = h + mamba2_bidir_mixer(u, ssm_w_in[j], ssm_conv_w[j], ssm_conv_b[j], ssm_dt_bias[j],
                                       ssm_A_log[j], ssm_D[j], ssm_norm_w[j], ssm_w_out[j])
        else:
            h = h + natten_mixer(u, na_w_in[j], na_rpb[j], na_w_out[j])
    return rmsnorm(h, final_norm_w)


_drawn_inputs = setup_inputs


def setup_inputs(seed=0):
    import zlib

    import numpy as np

    out = dict(_drawn_inputs(seed))
    spreads = {}
    factors = {}
    for name, (base, spread) in spreads.items():
        noise = np.random.default_rng([zlib.crc32(name.encode()), seed]).standard_normal(out[name].shape)
        drawn = base * np.exp(spread * noise) if base else spread * noise
        out[name] = __import__('jax').numpy.asarray(drawn.astype(out[name].dtype))
    for name, factor in factors.items():
        out[name] = (out[name] * factor).astype(out[name].dtype)
    return out
```

```python
from contextlib import ExitStack

import concourse.bass as bass
from concourse import mybir

F32 = mybir.dt.float32
F32R = mybir.dt.float32r
ACT = mybir.ActivationFunctionType
ALU = mybir.AluOpType

P = 128
SEQ = 256
NT = SEQ // P
DM = 2048
DI = 4096
KM, KI = DM // P, DI // P
GROUPS = 8
GH = 8
HP = 64
TAPS = 7
NB = 512
GRID_W = 64
GRID_H = SEQ // GRID_W
HD = 128
AH = 4
EPS = 1e-5
COL_Z, COL_X, COL_B, COL_C, COL_DT = 0, DI, 2 * DI, 2 * DI + 1024, 2 * DI + 2048

SLAB = 1024
RING = 4
DT_SLABS = 2
SSM, OUT, NA, FIN = 20, 16, 32, 16
SSM0 = DT_SLABS
OUT0 = SSM0 + GROUPS * SSM
NA0 = OUT0 + 4 * OUT
FIN0 = NA0 + GROUPS * NA

A_HI, A_LO, DT, XOFF_SC, Y_SC, SKIP, NPAR = 0, 4, 8, 12, 14, 16, 17
LE, GE, GT, LT = range(4)


def wait(eng, sem, value):
    if isinstance(value, int) and value <= 0:
        return
    eng.wait_ge(sem, value)


def bidir_hybrid(nc, x, norm_w, final_w, ssm_w_in, conv_wb, dt_bias, a_log, ssm_d, ssm_nw, ssm_w_out,
                 na_w_in, rpb_rows, na_w_out, c_ident, c_tri, c_win, out):
    with ExitStack() as ctx:
        def sb(name, shape, dt=F32):
            return ctx.enter_context(nc.sbuf_tensor(name, shape, dt))

        def sem(name):
            return ctx.enter_context(nc.semaphore(name))

        raw = sb("raw", [P, RING, SLAB])
        w_hi = sb("w_hi", [P, RING, SLAB], F32R)
        w_lo = sb("w_lo", [P, RING, SLAB], F32R)
        uT_hi = sb("uT_hi", [P, KM, SEQ], F32R)
        uT_lo = sb("uT_lo", [P, KM, SEQ], F32R)
        yT_hi = sb("yT_hi", [P, KI, SEQ], F32R)
        yT_lo = sb("yT_lo", [P, KI, SEQ], F32R)
        ident = sb("ident", [P, P])
        tri = sb("tri", [P, 4, P], F32R)
        nw = sb("nw", [P, 2, KM])
        snw = sb("snw", [P, KI])
        cw = sb("cw", [P, 48, TAPS + 1])
        cwc = sb("cwc", [P, 6, TAPS + 1])
        par = sb("par", [P, GROUPS, NPAR * GH])
        cur = sb("cur", [P, NPAR, GH])
        a_parts = sb("a_parts", [P, 2, NT, 2 * 64], F32R)
        stat = sb("stat", [P, 64])
        front = sb("front", [P, NT * DM])
        h = front[:, :].rearrange("p (t n) -> p t n", t=NT)
        rawbc = front[:, 0:512].rearrange("p (t n) -> p t n", t=NT)
        rawx = front[:, 512:1536].rearrange("p (t n) -> p t n", t=NT)
        cacc = front[:, 1536:3072].rearrange("p (c n) -> p c n", c=6)
        ctanh = front[:, 3072:4096].rearrange("p (c n) -> p c n", c=4)
        work = sb("work", [P, 9984])
        va = sb("va", [P, 4, NB], F32R)
        kT_hi = sb("kT_hi", [P, 2, NB], F32R)

        def area(at, n, parts=NT):
            return work[:, at:at + n].rearrange("p (t n) -> p t n", t=parts)

        xs, wdt, ztanh, xoff = (area(1024 * i, 1024) for i in range(4))
        gz, yb = area(4096, 1024), area(5120, 1024)
        toff, ebuf = work[:, 6144:6656], work[:, 6656:7168]
        scan = area(7168, 2048, 4)
        cbf, cbb, cbo = area(9216, 256), area(9472, 256), area(9728, 256)
        qs, ks, vt, agz = (area(1024 * i, 1024) for i in (0, 1, 4, 5))
        qT_lo, kT_lo = va[:, 0:2, :], va[:, 2:4, :]
        qT_hi = (tri[:, :, :].rearrange("p m n -> p (m n)"),
                 a_parts[:, :, :, :].rearrange("p a t n -> p (a t n)"))
        win = work[:, 9728:9984]
        atanh = qs
        bias, sc, pT = area(6144, 1024), area(7168, 1024), work[:, 8192:8704]
        hcur, junk = area(8704, 1024), work[:, 7168:7680]
        fw = work[:, 0:DM]
        dtv, dta, dte, brow, arow = (work[:, 256 * i:256 * (i + 1)] for i in range(5))
        dexp = work[:, 1536:1792]
        tri_in = work[:, 2048:2560]
        drow = work[:, 2560:2624]
        dt_turned = work[:, 2624:2880]
        junk2 = area(4096, NT * DM)
        SS, MS, RSTD, RHALF = 0, 2, 4, 6
        YSS, YCUR, YR = 8, 10, 12
        HSS, HCUR, HQ = 14, 16, 18
        MX, NMX, DEN, RDEN = 24, 28, 32, 40
        def st(c, n=1):
            return stat[:, c:c + n]

        bank = [ctx.enter_context(nc.psum_tensor(f"bank{i}", [P, NB], F32)) for i in range(8)]
        TR, XP, YA = bank[5], bank[6], bank[7]

        raw_full = [sem(f"raw_full{i}") for i in range(RING)]
        hi_ready, lo_ready, slab_used = sem("hi_ready"), sem("lo_ready"), sem("slab_used")
        x_loaded = [sem(f"x_loaded{i}") for i in range(4)]
        ident_loaded, nw_loaded, par_loaded = sem("ident_loaded"), sem("nw_loaded"), sem("par_loaded")
        table_ready, dtt_evac, dtt_back = sem("table_ready"), sem("dtt_evac"), sem("dtt_back")
        xt0_ready, u_hi_ready, u_lo_ready = sem("xt0_ready"), sem("u_hi_ready"), sem("u_lo_ready")
        tri_ready, sq_ready, ms_ready, rt_ready, rstd_ready = (
            sem(n) for n in ("tri_ready", "sq_ready", "ms_ready", "rt_ready", "rstd_ready"))
        dt_evac, dt_act, dt_dve, ap_ready, dec_ready, dexp_ready, par_ready = (
            sem(n) for n in ("dt_evac", "dt_act", "dt_dve", "ap_ready", "dec_ready", "dexp_ready", "par_ready"))
        cw_ready, cw_staged, par_staged = sem("cw_ready"), sem("cw_staged"), sem("par_staged")
        bc_evac, x_evac, z_evac = sem("bc_evac"), sem("x_evac"), sem("z_evac")
        bct_ready, xt_ready, xback_ready = sem("bct_ready"), sem("xt_ready"), sem("xback_ready")
        conv_init, conv_tap, ctanh_ready, conv_out = (
            sem(n) for n in ("conv_init", "conv_tap", "ctanh_ready", "conv_out"))
        cb_done, cb_evac, gz_ready, xs_evac = sem("cb_done"), sem("cb_evac"), sem("gz_ready"), sem("xs_evac")
        va_ready, xp_done, e_ready, m_ready = sem("va_ready"), sem("xp_done"), sem("e_ready"), sem("m_ready")
        xoff_ready, skip_ready, wdt_half = sem("xoff_ready"), sem("skip_ready"), sem("wdt_half")
        wdt_ready = sem("wdt_ready")
        yoff_done, toff_ready, ypart_ready, ydiag_done = (
            sem(n) for n in ("yoff_done", "toff_ready", "ypart_ready", "ydiag_done"))
        ysum_ready, y_ready, ysq_ready, yss_ready = (
            sem(n) for n in ("ysum_ready", "y_ready", "ysq_ready", "yss_ready"))
        yt_ready, yt_hi_ready, yt_lo_ready = sem("yt_ready"), sem("yt_hi_ready"), sem("yt_lo_ready")
        yr_ready, x_again, o_first, o_evac, h_kept, hsq_ready, hss_ready, ht_ready, ht_hi, ht_lo = (
            sem(n) for n in ("yr_ready", "x_again", "o_first", "o_evac", "h_kept", "hsq_ready", "hss_ready",
                             "ht_ready", "ht_hi", "ht_lo"))
        q_evac, k_evac, v_evac, g_evac = sem("q_evac"), sem("k_evac"), sem("v_evac"), sem("g_evac")
        qt_ready, kt_ready, qt_hi, qt_lo, kt_hi, kt_lo = (
            sem(n) for n in ("qt_ready", "kt_ready", "qt_hi", "qt_lo", "kt_hi", "kt_lo"))
        bias_full = [sem("bias_full0"), sem("bias_full1")]
        bias_ready, s_done, smax, smax_ready, p_ready = (
            sem(n) for n in ("bias_ready", "s_done", "smax", "smax_ready", "p_ready"))
        pt_ready, pt_evac, pv_done, agz_ready, rden_ready, rgz_ready, ao_ready = (
            sem(n) for n in ("pt_ready", "pt_evac", "pv_done", "agz_ready", "rden_ready", "rgz_ready", "ao_ready"))
        ot_ready, ot_hi, ot_lo = sem("ot_ready"), sem("ot_hi"), sem("ot_lo")
        win_loaded = sem("win_loaded")
        f_first, f_evac, fsq_ready, fw_loaded, fin_ready, stored = (
            sem(n) for n in ("f_first", "f_evac", "fsq_ready", "fw_loaded", "fin_ready", "stored"))

        DT_TURN0 = 9

        def slot(j):
            return (DT_SLABS + j) % RING

        def loads(phase, it, j):
            first = 1 if slot(j) < DT_SLABS else 0
            if phase == SSM0:
                return first + 6 * it + 2 + j // RING
            if phase == OUT0:
                return first + 6 * GROUPS + 4 * it + j // RING + 1
            if phase == NA0:
                return first + 6 * GROUPS + 16 + 8 * it + j // RING + 1
            return first + 6 * GROUPS + 16 + 8 * GROUPS + 4 * it + j // RING + 1

        def count(phase, it, j):
            per = {SSM0: SSM, OUT0: OUT, NA0: NA, FIN0: FIN}[phase]
            return phase + per * it + j + 1

        def act_slab(n, s, loaded):
            nc.scalar.wait_ge(raw_full[s], 16 * loaded)
            if not isinstance(n, int) or n > RING:
                nc.scalar.wait_ge(slab_used, n - RING)
            nc.scalar.activation(w_hi[:, s, :], raw[:, s, :], ACT.Copy).then_inc(hi_ready, 1)

        def dve_slab(n, s):
            nc.vector.wait_ge(hi_ready, n)
            nc.vector.tensor_tensor(w_lo[:, s, :], raw[:, s, :], w_hi[:, s, :].bitcast(F32),
                                    ALU.subtract).then_inc(lo_ready, 1)

        def pe_slab(n, s, act_hi, act_lo, kt0, kts, width, outs, first, last, shared=False, tile_free=None,
                    first_done=None):
            pe = nc.tensor
            pe.wait_ge(lo_ready, n)
            for t in range(NT):
                if tile_free is not None:
                    wait(pe, tile_free[0], tile_free[1] + t)
                for k in range(kts):
                    col = slice(k * width, (k + 1) * width)
                    a_h = act_hi[:, kt0 + k, t * P:(t + 1) * P]
                    a_l = act_lo[:, kt0 + k, t * P:(t + 1) * P]
                    opens = first and k == 0 and not (shared and t == 1)
                    closes = last and k == kts - 1
                    pe.matmul(outs[t], a_h, w_hi[:, s, col], start=opens, stop=False, skip_group_check=True)
                    pe.matmul(outs[t], a_h, w_lo[:, s, col], start=False, stop=False, skip_group_check=True)
                    mm = pe.matmul(outs[t], a_l, w_hi[:, s, col], start=False, stop=closes,
                                   skip_group_check=True)
                if t == 0 and first_done is not None:
                    mm.then_inc(first_done, 1)
            mm.then_inc(slab_used, 1)

        w1 = ssm_w_in.rearrange("(k p) n -> p k n", p=P)
        w2 = ssm_w_out.rearrange("(k p) n -> p k n", p=P)
        w3 = na_w_in.rearrange("(k p) n -> p k n", p=P)
        w4 = na_w_out.rearrange("(k p) n -> p k n", p=P)
        x_v = x.rearrange("(t p) n -> p t n", p=P)
        out_v = out.rearrange("(t p) n -> p t n", p=P)

        block = ctx.enter_context(nc.Block())

        @block.sync
        def _(sp):
            def free(n):
                if not isinstance(n, int) or n > RING:
                    sp.wait_ge(lo_ready, n - RING)

            def load(n, s, src, k0, kts, cols, waits_for=1):
                if waits_for:
                    free(n + waits_for - 1)
                sp.dma_start(raw[:, s, :].rearrange("p (k n) -> p k n", k=kts),
                             src[:, k0:k0 + kts, cols]).then_inc(raw_full[s], 16)

            def parameters():
                for dst, src in ((tri_in, c_tri), (snw[:, :], ssm_nw),
                                 (cw[:, :, :].rearrange("p c k -> p (c k)"), conv_wb),
                                 (brow[:, 0:P], dt_bias.partition_broadcast(P)),
                                 (arow[:, 0:P], a_log.partition_broadcast(P)),
                                 (drow, ssm_d.partition_broadcast(P))):
                    sp.dma_start(dst, src).then_inc(par_loaded, 16)

            def ssm_slabs(it):
                for j in range(SSM):
                    n, s = count(SSM0, it, j), slot(j)
                    if j == RING - DT_SLABS and isinstance(it, int):
                        parameters()
                    if j < 4:
                        free(n)
                        for half, col in enumerate((COL_B, COL_C)):
                            sp.dma_start(
                                raw[:, s, :].rearrange("p (k h n) -> p k h n", k=4, h=2)[:, :, half, :],
                                w1[:, 4 * j:4 * j + 4, bass.ds(it * P + col, P)]).then_inc(raw_full[s], 16)
                    elif j < 12:
                        load(n, s, w1, 2 * (j - 4), 2, bass.ds(it * NB + COL_X, NB), 2 if j == 11 else 1)
                    else:
                        load(n, s, w1, 2 * (j - 12), 2, bass.ds(it * NB + COL_Z, NB), 0 if j == 12 else 1)

            def load_bias(c, hh):
                k = AH * c + hh
                row = k * GRID_W if isinstance(k, int) else sp.snap(k * GRID_W)
                if not isinstance(k, int) or k >= 2:
                    sp.wait_ge(smax_ready, k - 1)
                for r in range(GRID_H):
                    t, half = r // 2, r % 2
                    sp.dma_start(bias[half * GRID_W:(half + 1) * GRID_W, hh % 2, t * SEQ:(t + 1) * SEQ],
                                 rpb_rows[bass.ds(row, GRID_W), (3 - r) * GRID_W:(7 - r) * GRID_W]
                                 ).then_inc(bias_full[hh % 2], 16)

            def na_slabs(it, prev):
                for j in range(NA):
                    load(count(NA0, it, j), slot(j), w3, 2 * (j % 8), 2,
                         bass.ds(it * NB + (j // 8) * DI, NB))
                    if j in (28, 31):
                        load_bias(it, (j - 28) // 3)
                    if j in (2, 5) and prev is not None:
                        load_bias(prev, 2 + (j - 2) // 3)

            sp.dma_start(ident[:, :], c_ident).then_inc(ident_loaded, 16)
            for i in range(4):
                cols = slice(i * NB, (i + 1) * NB)
                sp.dma_start(h[:, :, cols], x_v[:, :, cols]).then_inc(x_loaded[i], 16)
                if i == 0:
                    sp.dma_start(nw[:, :, :], norm_w).then_inc(nw_loaded, 16)
            for j in range(DT_SLABS):
                sp.dma_start(raw[:, j, :].rearrange("p (k n) -> p k n", k=8),
                             w1[:, 8 * j:8 * j + 8, COL_DT:COL_DT + P]).then_inc(raw_full[j], 16)
            ssm_slabs(0)
            with sp.Fori(1, GROUPS) as g:
                ssm_slabs(g)
            for j in range(OUT):
                load(count(OUT0, 0, j), slot(j), w2, 2 * j, 2, slice(0, NB))
                if j == 14:
                    sp.wait_ge(yoff_done, 2 * GROUPS)
                    sp.dma_start(win, c_win).then_inc(win_loaded, 16)
                if j == 10:
                    sp.wait_ge(xback_ready, 2 * GROUPS)
                    for t in range(NT):
                        sp.dma_start(h[:, t, :], x_v[:, t, :]).then_inc(x_again, 16)
            with sp.Fori(1, 4) as nb:
                for j in range(OUT):
                    load(count(OUT0, nb, j), slot(j), w2, 2 * j, 2, bass.ds(nb * NB, NB))
            na_slabs(0, None)
            with sp.Fori(1, GROUPS) as g:
                na_slabs(g, g - 1)
            for j in range(FIN):
                load(count(FIN0, 0, j), slot(j), w4, 2 * j, 2, slice(0, NB))
                if j in (2, 5):
                    load_bias(GROUPS - 1, 2 + (j - 2) // 3)
                if j == 14:
                    sp.wait_ge(agz_ready, NT * GROUPS)
                    sp.dma_start(fw, final_w.partition_broadcast(P)).then_inc(fw_loaded, 16)
            with sp.Fori(1, 4) as nb:
                for j in range(FIN):
                    load(count(FIN0, nb, j), slot(j), w4, 2 * j, 2, bass.ds(nb * NB, NB))
            for i in range(4):
                for t in range(NT):
                    sp.wait_ge(fin_ready, NT * i + t + 1)
                    sp.dma_start(out_v[:, t, i * NB:(i + 1) * NB],
                                 h[:, t, i * NB:(i + 1) * NB]).then_inc(stored, 16)
            sp.wait_ge(stored, 16 * 4 * NT)

        @block.tensor
        def _(pe):
            def transpose(dst, src):
                return pe.transpose(dst, src, ident[:, :])

            def ssm_slab(it, j):
                n, s = count(SSM0, it, j), slot(j)
                if j < 4:
                    if j == 0:
                        if not isinstance(it, int):
                            pe.wait_ge(bc_evac, it)
                    pe_slab(n, s, uT_hi, uT_lo, 4 * j, 4, 2 * P,
                            [bank[0][:, t * 2 * P:(t + 1) * 2 * P] for t in range(NT)], j == 0, j == 3,
                            shared=True)
                elif j < 12:
                    if j == 4:
                        wait(pe, x_evac, it)
                    pe_slab(n, s, uT_hi, uT_lo, 2 * (j - 4), 2, NB, [bank[1][:, :], bank[2][:, :]],
                            j == 4, j == 11)
                else:
                    if j == 12:
                        wait(pe, z_evac, it)
                    pe_slab(n, s, uT_hi, uT_lo, 2 * (j - 12), 2, NB, [bank[3][:, :], bank[4][:, :]],
                            j == 12, j == 19)

            def x_turn(q, r):
                for i in range(2):
                    for t in range(NT):
                        c = 2 * r + i
                        m = transpose((TR, YA)[r][:, i * SEQ + t * P:i * SEQ + (t + 1) * P],
                                      rawx[:, t, c * P:(c + 1) * P])
                m.then_inc(xt_ready, 1)

            def exponents(q, b):
                pe.wait_ge(va_ready, q * 4 + b + 1)
                if b > 0:
                    pe.wait_ge(e_ready, q * 4 + b)
                for i in range(4):
                    m = pe.matmul(XP[:, :], tri[:, GT if i < 2 else LT, :], va[:, i, :], start=(i == 0), stop=(i == 3))
                m.then_inc(xp_done, 1)

            def y_off(q, t):
                pe.wait_ge(xoff_ready, q * 2 + NT - t)
                if t == 0:
                    pe.wait_ge(e_ready, q * 4 + 4)
                else:
                    pe.wait_ge(toff_ready, q * 2 + 1)
                pe.matmul(XP[:, :], cbo[:, 1 - t, :], xoff[:, 1 - t, :], start=True, stop=True).then_inc(yoff_done, 1)

            def y_diag(q, t):
                pe.wait_ge(m_ready, q * 4 + 2 * t + 2)
                if t == 0:
                    pe.wait_ge(xs_evac, q * 2 + 2)
                else:
                    pe.wait_ge(ysum_ready, q * 2 + 1)
                for i in range(GH):
                    cols = slice(i * HP, (i + 1) * HP)
                    m = pe.matmul(YA[:, cols], scan[:, 2 * t + i // 4, (i % 4) * P:(i % 4 + 1) * P], xs[:, t, cols],
                                  start=True, stop=True)
                m.then_inc(ydiag_done, 1)

            def ssm_step(j, q):
                if j == 5:
                    pe.wait_ge(bc_evac, q + 1)
                    wait(pe, xs_evac, q * 2)
                    for c in range(2):
                        for t in range(NT):
                            m = transpose(TR[:, c * SEQ + t * P:c * SEQ + (t + 1) * P], rawbc[:, t, c * P:(c + 1) * P])
                    m.then_inc(bct_ready, 1)
                if j == 10:
                    pe.wait_ge(conv_out, q * 3 + 1)
                    for t in range(NT):
                        m = pe.matmul(TR[:, t * SEQ:(t + 1) * SEQ], cacc[:, 0, t * P:(t + 1) * P], cacc[:, 1, :],
                                      start=True, stop=True)
                    m.then_inc(cb_done, 1)
                if j == 13:
                    pe.wait_ge(x_evac, q + 1)
                    pe.wait_ge(cb_evac, q + 1)
                    wait(pe, yt_lo_ready, q * 4)
                    x_turn(q, 0)
                    x_turn(q, 1)
                if j == 15:
                    exponents(q, 0)
                if j == 17:
                    exponents(q, 1)
                if j == 19:
                    exponents(q, 2)
                if j == 21:
                    pe.wait_ge(conv_out, q * 3 + 3)
                    for t in range(NT):
                        for c in range(4):
                            m = transpose((TR, YA)[t][:, c * P:(c + 1) * P], cacc[:, 2 + c, t * P:(t + 1) * P])
                        m.then_inc(xback_ready, 1)
                if j == 22:
                    exponents(q, 3)
                if j == 23:
                    y_diag(q, 0)
                if j == 24:
                    y_off(q, 0)
                if j == 26:
                    y_off(q, 1)
                if j == 27:
                    y_diag(q, 1)
                if j == 30:
                    pe.wait_ge(y_ready, q * 2 + 2)
                    for c in range(4):
                        for t in range(NT):
                            at = (c % 2) * SEQ + t * P
                            m = transpose((YA, XP)[c // 2][:, at:at + P], yb[:, t, c * P:(c + 1) * P])
                        if c % 2:
                            m.then_inc(yt_ready, 1)

            def out_slab(nb, j):
                free = None
                if j == 0:
                    if isinstance(nb, int):
                        pe.wait_ge(x_evac, GROUPS)
                    else:
                        free = (o_evac, nb * 2 - 1)
                if isinstance(nb, int):
                    pe.wait_ge(yt_lo_ready, 2 * j + 2)
                pe_slab(count(OUT0, nb, j), slot(j), yT_hi, yT_lo, 2 * j, 2, NB, [bank[1][:, :], bank[2][:, :]],
                        j == 0, j == OUT - 1, tile_free=free, first_done=o_first if j == OUT - 1 else None)

            def out_step(j, nb):
                if j == 17:
                    pe.wait_ge(o_evac, nb * 2 + 2)
                    for c in range(4):
                        for t in range(NT):
                            at = (c % 2) * SEQ + t * P
                            m = transpose((TR, XP)[c // 2][:, at:at + P], hcur[:, t, c * P:(c + 1) * P])
                        if c % 2:
                            m.then_inc(ht_ready, 1)

            def na_slab(it, j):
                b = j // 8
                free = None
                if j % 8 == 0:
                    first = isinstance(it, int)
                    if b == 0:
                        if first:
                            free = (o_evac, 7)
                        else:
                            pe.wait_ge(v_evac, it)
                    if b == 1:
                        pe.wait_ge(z_evac, GROUPS) if first else pe.wait_ge(g_evac, it)
                    if b == 2:
                        pe.wait_ge(q_evac, it + 1)
                    if b == 3:
                        pe.wait_ge(k_evac, it + 1)
                if isinstance(it, int) and b == 0:
                    pe.wait_ge(ht_lo, 2 * j + 2)
                pe_slab(count(NA0, it, j), slot(j), uT_hi, uT_lo, 2 * (j % 8), 2, NB,
                        [bank[1 + 2 * (b % 2)][:, :], bank[2 + 2 * (b % 2)][:, :]], j % 8 == 0, j % 8 == 7,
                        tile_free=free)

            def head_turn(src, banks, done):
                for i in range(AH):
                    for t in range(NT):
                        at = (i % 2) * SEQ + t * P
                        m = transpose(banks[i // 2][:, at:at + P], src[:, t, i * HD:(i + 1) * HD])
                    if i % 2:
                        m.then_inc(done, 1)

            def na_step(j, q):
                if j == 18:
                    pe.wait_ge(q_evac, q + 1)
                    wait(pe, ot_lo, q * 4)
                    head_turn(qs, (bank[0], TR), qt_ready)
                if j == 20:
                    pe.wait_ge(k_evac, q + 1)
                    wait(pe, ao_ready, q * 2)
                    head_turn(ks, (XP, YA), kt_ready)
                for i in range(AH):
                    k = q * AH + i
                    if j == 25 + 3 * i:
                        pe.wait_ge(qt_lo, q * 2 + 2)
                        pe.wait_ge(kt_lo, q * 2 + 2)
                        if i > 0:
                            pe.wait_ge(smax, k * 2)
                        for t in range(NT):
                            at = (i % 2) * SEQ
                            q_t, k_t = slice(at + t * P, at + (t + 1) * P), slice(at, at + SEQ)
                            dst = bank[0][:, t * SEQ:(t + 1) * SEQ]
                            pe.matmul(dst, qT_hi[i // 2][:, q_t], kT_hi[:, i // 2, k_t], start=True, stop=False)
                            pe.matmul(dst, qT_hi[i // 2][:, q_t], kT_lo[:, i // 2, k_t], start=False, stop=False)
                            m = pe.matmul(dst, qT_lo[:, i // 2, q_t], kT_hi[:, i // 2, k_t], start=False, stop=True)
                        m.then_inc(s_done, 1)
                    if j == 28 + 3 * i:
                        pe.wait_ge(p_ready, k + 1)
                        if i > 0:
                            pe.wait_ge(pt_evac, k)
                        for kk in range(NT):
                            for t in range(NT):
                                m = transpose(TR[:, kk * SEQ + t * P:kk * SEQ + (t + 1) * P],
                                              sc[:, i % 2, t * SEQ + kk * P:t * SEQ + (kk + 1) * P])
                        m.then_inc(pt_ready, 1)
                    if j == 30 + 3 * i:
                        pe.wait_ge(pt_evac, k + 1)
                        if i == 0:
                            pe.wait_ge(v_evac, q + 1)
                        for t in range(NT):
                            for kk in range(NT):
                                m = pe.matmul((XP, YA)[t][:, i * HD:(i + 1) * HD],
                                              pT[:, kk * SEQ + t * P:kk * SEQ + (t + 1) * P],
                                              vt[:, kk, i * HD:(i + 1) * HD], start=(kk == 0), stop=(kk == 1))
                        m.then_inc(pv_done, 1)
                if j == 41:
                    pe.wait_ge(ao_ready, q * 2 + 2)
                    pe.wait_ge(pt_evac, q * AH + AH)
                    head_turn(agz, (bank[0], TR), ot_ready)

            def fin_slab(nb, j):
                free = None
                if j == 0:
                    if isinstance(nb, int):
                        pe.wait_ge(v_evac, GROUPS)
                    else:
                        free = (f_evac, nb * 2 - 1)
                if isinstance(nb, int):
                    pe.wait_ge(ot_lo, 2 * j + 2)
                pe_slab(count(FIN0, nb, j), slot(j), yT_hi, yT_lo, 2 * j, 2, NB, [bank[1][:, :], bank[2][:, :]],
                        j == 0, j == FIN - 1, tile_free=free, first_done=f_first if j == FIN - 1 else None)

            pe.wait_ge(ident_loaded, 16)
            for c in range(KM):
                if c % 4 == 0:
                    pe.wait_ge(x_loaded[c // 4], 16)
                for t in range(NT):
                    at = (c % 2) * SEQ + t * P
                    m = transpose(bank[c // 2][:, at:at + P], h[:, t, c * P:(c + 1) * P])
                if c % 2:
                    m.then_inc(xt0_ready, 1)
            for j in range(DT_SLABS):
                pe.wait_ge(lo_ready, j + 1)
                for k in range(8):
                    kt, dtt, w = 8 * j + k, bank[1][:, 0:SEQ], slice(k * P, (k + 1) * P)
                    pe.wait_ge(u_lo_ready, max(kt + 1, 4))
                    pe.matmul(dtt, w_hi[:, j, w], uT_hi[:, kt, :], start=(kt == 0), stop=False,
                              skip_group_check=True)
                    pe.matmul(dtt, w_lo[:, j, w], uT_hi[:, kt, :], start=False, stop=False,
                              skip_group_check=True)
                    m = pe.matmul(dtt, w_hi[:, j, w], uT_lo[:, kt, :], start=False, stop=(kt == KM - 1),
                                  skip_group_check=True)
                m.then_inc(slab_used, 1)
            for j in range(SSM):
                ssm_slab(0, j)
                if j == 1:
                    pe.wait_ge(dtt_evac, 1)
                    for t in range(NT):
                        m = transpose(XP[:, t * P:(t + 1) * P], dt_turned[:, t * P:(t + 1) * P])
                    m.then_inc(dtt_back, 1)
                if j == 6:
                    pe.wait_ge(ap_ready, 2)
                    for i, (m_, t, d) in enumerate(((LE, 1, 0), (GT, 0, 0), (GE, 0, 1), (LT, 1, 1))):
                        for part in range(2):
                            m = pe.matmul(XP[:, i * 64:(i + 1) * 64], tri[:, m_, :],
                                          a_parts[:, part, t, d * 64:(d + 1) * 64], start=(part == 0), stop=(part == 1))
                    m.then_inc(dec_ready, 1)
                ssm_step(j, 0)
            with pe.Fori(1, GROUPS) as g:
                for j in range(SSM):
                    ssm_slab(g, j)
                    ssm_step(SSM + j, g - 1)
                    ssm_step(j, g)
            for j in range(OUT):
                out_slab(0, j)
                ssm_step(SSM + j, GROUPS - 1)
            with pe.Fori(1, 4) as nb:
                for j in range(OUT):
                    out_slab(nb, j)
                    out_step(OUT + j, nb - 1)
            for j in range(NA):
                na_slab(0, j)
                out_step(OUT + j, 3)
                na_step(j, 0)
            with pe.Fori(1, GROUPS) as g:
                for j in range(NA):
                    na_slab(g, j)
                    na_step(NA + j, g - 1)
                    na_step(j, g)
            for j in range(FIN):
                fin_slab(0, j)
                na_step(NA + j, GROUPS - 1)
            with pe.Fori(1, 4) as nb:
                for j in range(FIN):
                    fin_slab(nb, j)

        @block.scalar
        def _(act):
            def root():
                return nc.scalar.activation(st(MS, 2), st(MS, 2), ACT.Sqrt)

            def conv_start(q, banks, first, which):
                for i in range(2):
                    m = nc.scalar.activation(cacc[:, first + i, :], banks[:, i * SEQ:(i + 1) * SEQ], ACT.Identity,
                                             scale=cwc[:, first + i, 3:4], bias=cwc[:, first + i, TAPS:TAPS + 1])
                m.then_inc(conv_init, 1)

            def conv_tanh(q, first, at, which):
                act.wait_ge(conv_tap, q * 36 + 12 * (which + 1))
                if which != 1:
                    wait(act, conv_out, q * 3 + which)
                nc.scalar.activation(ctanh[:, at:at + 2, :], cacc[:, first:first + 2, :], ACT.Tanh
                                     ).then_inc(ctanh_ready, 1)

            def ssm_step(j, q):
                if j == 7:
                    act.wait_ge(slab_used, count(SSM0, q, 3))
                    for t in range(NT):
                        m = nc.scalar.activation(rawbc[:, t, :], bank[0][:, t * 2 * P:(t + 1) * 2 * P], ACT.Copy,
                                                 scale=st(RSTD + t))
                    m.then_inc(bc_evac, 1)
                if j == 9:
                    act.wait_ge(bct_ready, q + 1)
                    act.wait_ge(cw_staged, q + 1)
                    conv_start(q, TR, 0, 0)
                if j == 11:
                    conv_tanh(q, 0, 0, 0)
                if j == 15:
                    act.wait_ge(slab_used, count(SSM0, q, 11))
                    for t in range(NT):
                        m = nc.scalar.activation(rawx[:, t, :], bank[1 + t][:, :], ACT.Copy, scale=st(RSTD + t))
                    m.then_inc(x_evac, 1)
                if j == 17:
                    wait(act, xback_ready, q * 2)
                    act.wait_ge(xt_ready, q * 2 + 1)
                    conv_start(q, TR, 2, 1)
                    act.wait_ge(xt_ready, q * 2 + 2)
                    conv_start(q, YA, 4, 2)
                if j == 19:
                    exp_x(q, 0)
                if j == 20:
                    conv_tanh(q, 2, 2, 1)
                if j == 21:
                    exp_x(q, 1)
                if j == 22:
                    conv_tanh(q, 4, 0, 2)
                if j == 23:
                    exp_x(q, 2)
                    act.wait_ge(slab_used, count(SSM0, q, 19))
                    for t in range(NT):
                        nc.scalar.activation(gz[:, t, :], bank[3 + t][:, :], ACT.Copy, scale=st(RHALF + t))
                        m = nc.scalar.activation(ztanh[:, t, :], bank[3 + t][:, :], ACT.Tanh, scale=st(RHALF + t))
                    m.then_inc(z_evac, 1)
                if j == 24:
                    for t in range(NT):
                        act.wait_ge(xback_ready, q * 2 + t + 1)
                        nc.scalar.activation(xs[:, t, :], (TR, YA)[t][:, :], ACT.Copy).then_inc(xs_evac, 1)
                if j == 26:
                    exp_x(q, 3)
                if j == 33:
                    for t in range(NT):
                        act.wait_ge(y_ready, q * 2 + t + 1)
                        act.wait_ge(m_ready, q * 4 + 4)
                        if t:
                            act.wait_ge(ysq_ready, q * 2 + t)
                        nc.scalar.activation(ebuf, yb[:, t, :], ACT.Square, accum_out=st(YCUR + t)
                                             ).then_inc(ysq_ready, 1)
                    for c in range(4):
                        act.wait_ge(yt_ready, q * 2 + c // 2 + 1)
                        nc.scalar.activation(yT_hi[:, bass.ds(q * 4 + c, 1), :], (YA, XP)[c // 2][:, (c % 2) * SEQ:
                                             (c % 2 + 1) * SEQ].unsqueeze(1), ACT.Copy,
                                             scale=snw[:, bass.ds(q * 4 + c, 1)]).then_inc(yt_hi_ready, 1)

            def exp_x(q, b):
                act.wait_ge(xp_done, q * 4 + b + 1)
                if b == 0:
                    wait(act, ysq_ready, q * 2)
                wait(act, m_ready, q * 4 + b)
                nc.scalar.activation(ebuf, XP[:, :], ACT.Exp).then_inc(e_ready, 1)

            def out_step(j, nb):
                if j == 19:
                    for t in range(NT):
                        act.wait_ge(o_evac, nb * 2 + t + 1)
                        act.wait_ge(hss_ready, nb + 1)
                        if t:
                            act.wait_ge(hsq_ready, nb * 2 + t)
                        nc.scalar.activation(junk, hcur[:, t, :], ACT.Square, accum_out=st(HCUR + t)
                                             ).then_inc(hsq_ready, 1)
                if j == 20:
                    for c in range(4):
                        act.wait_ge(ht_ready, nb * 2 + c // 2 + 1)
                        nc.scalar.activation(uT_hi[:, bass.ds(nb * 4 + c, 1), :], (TR, XP)[c // 2][:, (c % 2) * SEQ:
                                             (c % 2 + 1) * SEQ].unsqueeze(1), ACT.Copy,
                                             scale=nw[:, 1, bass.ds(nb * 4 + c, 1)]).then_inc(ht_hi, 1)

            def rows_out(dst, q, j_last, pair, scale, done):
                act.wait_ge(slab_used, count(NA0, q, j_last))
                for t in range(NT):
                    m = nc.scalar.activation(dst[:, t, :], bank[pair + t][:, :], ACT.Copy, scale=st(scale + t))
                m.then_inc(done, 1)

            def turned(dst, banks, ready, base, done):
                for i in range(2):
                    act.wait_ge(ready, base + i + 1)
                    nc.scalar.activation(dst[i], banks[i][:, :], ACT.Copy).then_inc(done, 1)

            def na_step(j, q):
                if j == 11:
                    wait(act, agz_ready, q * 2)
                    rows_out(qs, q, 7, 1, HQ, q_evac)
                if j == 19:
                    wait(act, kt_ready, q * 2)
                    rows_out(ks, q, 15, 3, RSTD, k_evac)
                if j == 22:
                    turned(qT_hi, (bank[0], TR), qt_ready, q * 2, qt_hi)
                if j == 24:
                    turned((kT_hi[:, 0, :], kT_hi[:, 1, :]), (XP, YA), kt_ready, q * 2, kt_hi)
                if j == 27:
                    wait(act, pv_done, q * AH)
                    rows_out(vt, q, 23, 1, RSTD, v_evac)
                if j == 35:
                    act.wait_ge(slab_used, count(NA0, q, 31))
                    for t in range(NT):
                        nc.scalar.activation(agz[:, t, :], bank[3 + t][:, :], ACT.Copy, scale=st(RHALF + t))
                        m = nc.scalar.activation(atanh[:, t, :], bank[3 + t][:, :], ACT.Tanh, scale=st(RHALF + t))
                    m.then_inc(g_evac, 1)
                for i in range(AH):
                    k = q * AH + i
                    if j == 30 + 3 * i:
                        act.wait_ge(smax_ready, k + 1)
                        for t in range(NT):
                            m = nc.scalar.activation(sc[:, i % 2, t * SEQ:(t + 1) * SEQ],
                                                     sc[:, i % 2, t * SEQ:(t + 1) * SEQ], ACT.Exp,
                                                     bias=st(NMX + 2 * (i % 2) + t), accum_out=st(DEN + 4 * t + i))
                        m.then_inc(p_ready, 1)
                    if j == 32 + 3 * i:
                        act.wait_ge(pt_ready, k + 1)
                        if i > 0:
                            act.wait_ge(pv_done, k)
                        nc.scalar.activation(pT, TR[:, :], ACT.Copy).then_inc(pt_evac, 1)
                if j == 45:
                    for c in range(4):
                        act.wait_ge(ot_ready, q * 2 + c // 2 + 1)
                        nc.scalar.activation(yT_hi[:, bass.ds(q * 4 + c, 1), :], (bank[0], TR)[c // 2][:, (c % 2) * SEQ:
                                             (c % 2 + 1) * SEQ].unsqueeze(1), ACT.Copy).then_inc(ot_hi, 1)

            def fin_step(j, nb):
                if j == 18:
                    for t in range(NT):
                        act.wait_ge(f_evac, nb * 2 + t + 1)
                        act.wait_ge(hss_ready, nb + 6)
                        if t:
                            act.wait_ge(fsq_ready, nb * 2 + t)
                        nc.scalar.activation(junk, h[:, t, bass.ds(nb * NB, NB)], ACT.Square,
                                             accum_out=st(HCUR + t)).then_inc(fsq_ready, 1)

            act.wait_ge(hss_ready, 1)
            nc.scalar.activation(st(HCUR), st(HSS), ACT.Copy).then_inc(table_ready, 1)
            act.wait_ge(nw_loaded, 16)
            for c in range(KM):
                act.wait_ge(xt0_ready, c // 2 + 1)
                nc.scalar.activation(uT_hi[:, c, :], bank[c // 2][:, (c % 2) * SEQ:(c % 2 + 1) * SEQ], ACT.Copy,
                                     scale=nw[:, 0, c:c + 1]).then_inc(u_hi_ready, 1)
                if c in (DT_TURN0, 15):
                    act_slab(1 + c // 15, c // 15, 1)
            for j in range(SSM):
                act_slab(count(SSM0, 0, j), slot(j), loads(SSM0, 0, j))
                if j in (1, 2):
                    nc.scalar.activation(junk2[:, j - 1, :], h[:, j - 1, :], ACT.Square, accum_out=st(SS + j - 1)
                                         ).then_inc(sq_ready, 1)
                if j == 3:
                    act.wait_ge(slab_used, DT_SLABS)
                    nc.scalar.activation(dt_turned, bank[1][:, 0:SEQ], ACT.Copy).then_inc(dtt_evac, 1)
                    act.wait_ge(ms_ready, 1)
                    root().then_inc(rt_ready, 1)
                    act.wait_ge(par_loaded, 16 * 6)
                    nc.scalar.activation(arow[:, 0:P], arow[:, 0:P], ACT.Exp).then_inc(dt_act, 1)
                if j == 5:
                    act.wait_ge(dt_evac, NT)
                    nc.scalar.activation(dte, dtv, ACT.Abs).then_inc(dt_act, 1)
                    act.wait_ge(dt_act, 2)
                    nc.scalar.activation(dte, dte, ACT.Exp, scale=-1.0).then_inc(dt_act, 1)
                if j == 6:
                    act.wait_ge(dt_dve, 1)
                    nc.scalar.activation(dte, dte, ACT.Ln).then_inc(dt_act, 1)
                if j == 10:
                    act.wait_ge(dec_ready, 1)
                    nc.scalar.activation(dexp, XP[:, 0:256], ACT.Exp).then_inc(dexp_ready, 1)
                ssm_step(j, 0)
            with act.Fori(1, GROUPS) as g:
                for j in range(SSM):
                    act_slab(count(SSM0, g, j), slot(j), loads(SSM0, g, j))
                    ssm_step(SSM + j, g - 1)
                    ssm_step(j, g)
            for j in range(OUT):
                act_slab(count(OUT0, 0, j), slot(j), loads(OUT0, 0, j))
                ssm_step(SSM + j, GROUPS - 1)
                if j == 15:
                    act.wait_ge(ms_ready, 2)
                    root().then_inc(rt_ready, 1)
            with act.Fori(1, 4) as nb:
                for j in range(OUT):
                    act_slab(count(OUT0, nb, j), slot(j), loads(OUT0, nb, j))
                    out_step(OUT + j, nb - 1)
            for j in range(NA):
                act_slab(count(NA0, 0, j), slot(j), loads(NA0, 0, j))
                out_step(OUT + j, 3)
                if j == 6:
                    act.wait_ge(ms_ready, 3)
                    root().then_inc(rt_ready, 1)
                if j == 11:
                    act.wait_ge(rstd_ready, 3)
                na_step(j, 0)
            with act.Fori(1, GROUPS) as g:
                for j in range(NA):
                    act_slab(count(NA0, g, j), slot(j), loads(NA0, g, j))
                    na_step(NA + j, g - 1)
                    na_step(j, g)
            for j in range(FIN):
                act_slab(count(FIN0, 0, j), slot(j), loads(FIN0, 0, j))
                na_step(NA + j, GROUPS - 1)
            with act.Fori(1, 4) as nb:
                for j in range(FIN):
                    act_slab(count(FIN0, nb, j), slot(j), loads(FIN0, nb, j))
                    fin_step(FIN + j, nb - 1)
            fin_step(18, 3)
            act.wait_ge(ms_ready, 4)
            root().then_inc(rt_ready, 1)

        @block.vector
        def _(dve):
            tt = nc.vector.tensor_tensor

            def mean_square(ss, n):
                nc.vector.tensor_scalar(st(MS, 2), st(ss, 2), 1.0 / n, EPS, ALU.mult, ALU.add).then_inc(ms_ready, 1)

            def heads(col, n=GH, first=0, width=HP):
                return cur[:, col, first:first + n].unsqueeze(2).to_broadcast([P, n, width])

            def by_head(ap, n=GH):
                return ap.rearrange("p (h w) -> p h w", h=n)

            def taps(q, bank_, first, which, half):
                if half == 0:
                    dve.wait_ge(conv_init, q * 3 + which + 1)
                n = 12 * which + 6 * half
                for k in ((0, 1, 2), (4, 5, 6))[half]:
                    lo, hi = max(0, 3 - k), min(SEQ, SEQ + 3 - k)
                    for i in range(2):
                        if k > 0:
                            dve.wait_ge(conv_tap, q * 36 + n - 1)
                        acc = cacc[:, first + i, lo:hi]
                        src = bank_[:, i * SEQ + lo + k - 3:i * SEQ + hi + k - 3]
                        nc.vector.scalar_tensor_tensor(acc, src, cwc[:, first + i, k:k + 1], acc, ALU.mult, ALU.add
                                                       ).then_inc(conv_tap, 1)
                        n += 1

            def silu(q, first, at, which):
                dve.wait_ge(ctanh_ready, q * 3 + which + 1)
                nc.vector.scalar_tensor_tensor(cacc[:, first:first + 2, :], ctanh[:, at:at + 2, :], 1.0,
                                               cacc[:, first:first + 2, :], ALU.add, ALU.mult).then_inc(conv_out, 1)

            def weights(q, b):
                t = b // 2
                w = wdt[:, b % 2, :]
                for i in range(4):
                    hh = 4 * (b % 2) + i
                    nc.vector.tensor_scalar(w[:, i * P:(i + 1) * P], cbf[:, t, :], cur[:, DT + 2 * t, hh:hh + 1],
                                            None, ALU.mult).then_inc(wdt_half, 1)
                for i in range(4):
                    hh = 4 * (b % 2) + i
                    dve.wait_ge(wdt_half, q * 16 + b * 4 + i + 1)
                    m = nc.vector.scalar_tensor_tensor(w[:, i * P:(i + 1) * P], cbb[:, t, :],
                                                       cur[:, DT + 2 * t + 1, hh:hh + 1], w[:, i * P:(i + 1) * P],
                                                       ALU.mult, ALU.add)
                m.then_inc(wdt_ready, 1)

            def m_products(q, b):
                dve.wait_ge(e_ready, q * 4 + b + 1)
                dve.wait_ge(wdt_ready, q * 4 + b + 1)
                tt(scan[:, b, :], ebuf, wdt[:, b % 2, :], ALU.mult).then_inc(m_ready, 1)

            def y_sum(q, t):
                dve.wait_ge(ydiag_done, q * 2 + t + 1)
                dve.wait_ge(ypart_ready, q * 2 + t + 1)
                tt(yb[:, t, :], YA[:, :], yb[:, t, :], ALU.add).then_inc(ysum_ready, 1)
                dve.wait_ge(ysum_ready, q * 2 + t + 1)
                dve.wait_ge(gz_ready, q + 1)
                tt(yb[:, t, :], yb[:, t, :], gz[:, t, :], ALU.mult).then_inc(y_ready, 1)

            def y_tile_off(q, t):
                dve.wait_ge(yoff_done, q * 2 + t + 1)
                if t == 1:
                    dve.wait_ge(ypart_ready, q * 2 + 1)
                tt(by_head(toff), by_head(XP[:, :]), heads(Y_SC + t), ALU.mult).then_inc(toff_ready, 1)

            def ssm_step(j, q):
                if j in (9, 10):
                    taps(q, TR, 0, 0, j - 9)
                if j == 12:
                    silu(q, 0, 0, 0)
                if j == 14:
                    dve.wait_ge(cb_done, q + 1)
                    wait(dve, yoff_done, q * 2)
                    for t in range(NT):
                        diag = TR[:, t * (SEQ + P):t * (SEQ + P) + P]
                        tt(cbf[:, t, :], diag, tri[:, LE, :].bitcast(F32), ALU.mult)
                        tt(cbb[:, t, :], diag, tri[:, GE, :].bitcast(F32), ALU.mult)
                    nc.vector.tensor_copy(work[:, 9728:9984], TR[:, P:P + SEQ]).then_inc(cb_evac, 1)
                if j == 15:
                    dve.wait_ge(cb_evac, q + 1)
                    dve.wait_ge(par_staged, q + 1)
                    weights(q, 0)
                if j == 16:
                    weights(q, 1)
                if j in (17, 18):
                    taps(q, TR, 2, 1, j - 17)
                if j in (19, 20):
                    taps(q, YA, 4, 2, j - 19)
                if j == 20:
                    m_products(q, 0)
                if j == 21:
                    silu(q, 2, 2, 1)
                if j == 22:
                    m_products(q, 1)
                if j == 23:
                    silu(q, 4, 0, 2)
                if j == 24:
                    weights(q, 2)
                    dve.wait_ge(z_evac, q + 1)
                    nc.vector.scalar_tensor_tensor(gz[:, :, :], ztanh[:, :, :], 1.0, gz[:, :, :], ALU.add, ALU.mult
                                                   ).then_inc(gz_ready, 1)
                if j == 25:
                    m_products(q, 2)
                    weights(q, 3)
                if j == 27:
                    m_products(q, 3)
                    y_tile_off(q, 0)
                if j == 28:
                    y_sum(q, 0)
                if j == 29:
                    y_tile_off(q, 1)
                if j == 31:
                    y_sum(q, 1)
                if j == 33:
                    for c in range(4):
                        dve.wait_ge(yt_hi_ready, q * 4 + c // 2 * 2 + 2)
                        kt = bass.ds(q * 4 + c, 1)
                        nc.vector.scalar_tensor_tensor(yT_lo[:, kt, :], (YA, XP)[c // 2][:, (c % 2) * SEQ:
                                                       (c % 2 + 1) * SEQ].unsqueeze(1), snw[:, kt],
                                                       yT_hi[:, kt, :].bitcast(F32), ALU.mult, ALU.subtract
                                                       ).then_inc(yt_lo_ready, 1)

            def out_step(j, nb):
                if j == 17:
                    for t in range(NT):
                        if t == 0:
                            dve.wait_ge(o_first, nb + 1)
                        else:
                            dve.wait_ge(slab_used, count(OUT0, nb, OUT - 1))
                        dve.wait_ge(hss_ready, nb + 1)
                        nc.vector.scalar_tensor_tensor(hcur[:, t, :], bank[1 + t][:, :], st(YR + t),
                                                       h[:, t, bass.ds(nb * NB, NB)], ALU.mult, ALU.add
                                                       ).then_inc(o_evac, 1)
                if j == 20:
                    for c in range(4):
                        dve.wait_ge(ht_hi, nb * 4 + c // 2 * 2 + 2)
                        kt = bass.ds(nb * 4 + c, 1)
                        nc.vector.scalar_tensor_tensor(uT_lo[:, kt, :], (TR, XP)[c // 2][:, (c % 2) * SEQ:
                                                       (c % 2 + 1) * SEQ].unsqueeze(1), nw[:, 1, kt],
                                                       uT_hi[:, kt, :].bitcast(F32), ALU.mult, ALU.subtract
                                                       ).then_inc(ht_lo, 1)

            def turned_lo(lo, hi, banks, ready, base, done):
                for i in range(2):
                    dve.wait_ge(ready, base + i + 1)
                    tt(lo[:, i, :], banks[i][:, :], hi[i].bitcast(F32), ALU.subtract).then_inc(done, 1)

            def na_step(j, q):
                if j == 23:
                    turned_lo(qT_lo, qT_hi, (bank[0], TR), qt_hi, q * 2, qt_lo)
                if j == 25:
                    turned_lo(kT_lo, (kT_hi[:, 0, :], kT_hi[:, 1, :]), (XP, YA), kt_hi, q * 2, kt_lo)
                for i in range(AH):
                    if j == 29 + 3 * i:
                        k = q * AH + i
                        dve.wait_ge(s_done, k + 1)
                        dve.wait_ge(bias_ready, k + 1)
                        if i > 1:
                            dve.wait_ge(pt_ready, k - 1)
                        m = 2 * (i % 2)
                        tt(sc[:, i % 2, :], bank[0][:, :], bias[:, i % 2, :], ALU.add).then_inc(smax, 1)
                        dve.wait_ge(smax, k * 2 + 1)
                        nc.vector.tensor_reduce(st(MX + m, 2), sc[:, i % 2, :].rearrange("p (t n) -> p t n", t=NT),
                                                mybir.AxisListType.X, ALU.max).then_inc(smax, 1)
                        dve.wait_ge(smax, k * 2 + 2)
                        nc.vector.tensor_scalar(st(NMX + m, 2), st(MX + m, 2), -1.0, None, ALU.mult
                                                ).then_inc(smax_ready, 1)
                if j == 36:
                    dve.wait_ge(g_evac, q + 1)
                    for t in range(NT):
                        nc.vector.scalar_tensor_tensor(agz[:, t, :], atanh[:, t, :], 1.0, agz[:, t, :], ALU.add,
                                                       ALU.mult).then_inc(agz_ready, 1)
                if j == 41:
                    dve.wait_ge(p_ready, q * AH + AH)
                    dve.wait_ge(agz_ready, q * 2 + 2)
                    nc.vector.reciprocal(st(RDEN, 8), st(DEN, 8)).then_inc(rden_ready, 1)
                    dve.wait_ge(rden_ready, q + 1)
                    for t in range(NT):
                        tt(by_head(agz[:, t, :], AH), by_head(agz[:, t, :], AH),
                           st(RDEN + 4 * t, 4).unsqueeze(2).to_broadcast([P, AH, HD]), ALU.mult).then_inc(rgz_ready, 1)
                if j == 42:
                    dve.wait_ge(pv_done, q * AH + AH)
                    for t in range(NT):
                        dve.wait_ge(rgz_ready, q * 2 + t + 1)
                        tt(agz[:, t, :], (XP, YA)[t][:, :], agz[:, t, :], ALU.mult).then_inc(ao_ready, 1)
                if j == 45:
                    for c in range(4):
                        dve.wait_ge(ot_hi, q * 4 + c // 2 * 2 + 2)
                        kt = bass.ds(q * 4 + c, 1)
                        tt(yT_lo[:, kt, :], (bank[0], TR)[c // 2][:, (c % 2) * SEQ:(c % 2 + 1) * SEQ].unsqueeze(1),
                           yT_hi[:, kt, :].bitcast(F32), ALU.subtract).then_inc(ot_lo, 1)

            def fin_step(j, nb):
                if j == 17:
                    for t in range(NT):
                        if t == 0:
                            dve.wait_ge(f_first, nb + 1)
                        else:
                            dve.wait_ge(slab_used, count(FIN0, nb, FIN - 1))
                        hn = h[:, t, bass.ds(nb * NB, NB)]
                        tt(hn, bank[1 + t][:, :], hn, ALU.add).then_inc(f_evac, 1)

            for c in range(KM):
                dve.wait_ge(u_hi_ready, c // 2 * 2 + 2)
                nc.vector.scalar_tensor_tensor(uT_lo[:, c, :], bank[c // 2][:, (c % 2) * SEQ:(c % 2 + 1) * SEQ],
                                               nw[:, 0, c:c + 1], uT_hi[:, c, :].bitcast(F32), ALU.mult, ALU.subtract
                                               ).then_inc(u_lo_ready, 1)
                if c in (DT_TURN0, 15):
                    dve_slab(1 + c // 15, c // 15)
            nc.vector.memset(st(YSS, 2), 0.0).then_inc(yss_ready, 1)
            for j in range(SSM):
                dve_slab(count(SSM0, 0, j), slot(j))
                if j == 2:
                    dve.wait_ge(sq_ready, NT)
                    mean_square(SS, DM)
                if j == 3:
                    dve.wait_ge(par_loaded, 16 * 6)
                    nc.vector.tensor_copy(tri[:, :, :].rearrange("p m n -> p (m n)"), tri_in).then_inc(tri_ready, 1)
                    nc.vector.tensor_scalar(cw[:, :, :], cw[:, :, :], 0.5, None, ALU.mult).then_inc(cw_ready, 1)
                    dve.wait_ge(rt_ready, 1)
                    nc.vector.reciprocal(st(RSTD, 2), st(MS, 2)).then_inc(rstd_ready, 1)
                    dve.wait_ge(rstd_ready, 1)
                    nc.vector.tensor_scalar(st(RHALF, 2), st(RSTD, 2), 0.5, None, ALU.mult).then_inc(rstd_ready, 1)
                if j == 4:
                    dve.wait_ge(dtt_back, 1)
                    for t in range(NT):
                        nc.vector.scalar_tensor_tensor(dtv[:, t * P:(t + 1) * P], XP[:, t * P:(t + 1) * P],
                                                       st(RSTD + t), brow[:, 0:P], ALU.mult, ALU.add
                                                       ).then_inc(dt_evac, 1)
                if j == 5:
                    dve.wait_ge(dt_act, 3)
                    nc.vector.tensor_scalar(dte, dte, 1.0, None, ALU.add).then_inc(dt_dve, 1)
                if j == 6:
                    dve.wait_ge(dt_act, 4)
                    nc.vector.scalar_tensor_tensor(dtv, dtv, 0.0, dte, ALU.max, ALU.add).then_inc(dt_dve, 1)
                    dve.wait_ge(dt_dve, 2)
                    v3 = dtv.rearrange("p (t n) -> p t n", t=NT)
                    a3 = dta.rearrange("p (t n) -> p t n", t=NT)
                    nc.vector.scalar_tensor_tensor(a3, v3, -1.0, arow[:, 0:P].unsqueeze(1).to_broadcast([P, NT, P]),
                                                   ALU.mult, ALU.mult).then_inc(dt_dve, 1)
                    dve.wait_ge(dt_dve, 3)
                    nc.vector.tensor_copy(a_parts[:, 0, :, :], a3).then_inc(ap_ready, 1)
                    dve.wait_ge(ap_ready, 1)
                    tt(a_parts[:, 1, :, :], a3, a_parts[:, 0, :, :].bitcast(F32), ALU.subtract).then_inc(ap_ready, 1)
                ssm_step(j, 0)
            with dve.Fori(1, GROUPS) as g:
                for j in range(SSM):
                    dve_slab(count(SSM0, g, j), slot(j))
                    ssm_step(SSM + j, g - 1)
                    ssm_step(j, g)
            for j in range(OUT):
                dve_slab(count(OUT0, 0, j), slot(j))
                ssm_step(SSM + j, GROUPS - 1)
                if j == 15:
                    dve.wait_ge(yss_ready, GROUPS + 1)
                    mean_square(YSS, DI)
            with dve.Fori(1, 4) as nb:
                for j in range(OUT):
                    dve_slab(count(OUT0, nb, j), slot(j))
                    if j == 0:
                        dve.wait_ge(rt_ready, 2)
                        nc.vector.reciprocal(st(YR, 2), st(MS, 2)).then_inc(yr_ready, 1)
                        dve.wait_ge(yr_ready, nb)
                        dve.wait_ge(x_again, 32)
                    out_step(OUT + j, nb - 1)
            for j in range(NA):
                dve_slab(count(NA0, 0, j), slot(j))
                out_step(OUT + j, 3)
                if j == 5:
                    dve.wait_ge(hss_ready, 5)
                    mean_square(HSS, DM)
                if j == 7:
                    dve.wait_ge(rt_ready, 3)
                    nc.vector.reciprocal(st(RSTD, 2), st(MS, 2)).then_inc(yr_ready, 1)
                    dve.wait_ge(yr_ready, 4)
                    nc.vector.tensor_scalar(st(RHALF, 2), st(RSTD, 2), 0.5, None, ALU.mult)
                    nc.vector.tensor_scalar(st(HQ, 2), st(RSTD, 2), float(HD) ** -0.5, None, ALU.mult
                                            ).then_inc(rstd_ready, 1)
                na_step(j, 0)
            with dve.Fori(1, GROUPS) as g:
                for j in range(NA):
                    dve_slab(count(NA0, g, j), slot(j))
                    na_step(NA + j, g - 1)
                    na_step(j, g)
            for j in range(FIN):
                dve_slab(count(FIN0, 0, j), slot(j))
                na_step(NA + j, GROUPS - 1)
            with dve.Fori(1, 4) as nb:
                for j in range(FIN):
                    dve_slab(count(FIN0, nb, j), slot(j))
                    fin_step(FIN + j, nb - 1)
            fin_step(17, 3)
            dve.wait_ge(hss_ready, 10)
            mean_square(HSS, DM)
            dve.wait_ge(rt_ready, 4)
            nc.vector.reciprocal(st(RSTD, 2), st(MS, 2)).then_inc(rstd_ready, 1)
            dve.wait_ge(rstd_ready, 4)
            dve.wait_ge(fw_loaded, 16)
            for i in range(4):
                for t in range(NT):
                    cols = slice(i * NB, (i + 1) * NB)
                    nc.vector.scalar_tensor_tensor(h[:, t, cols], h[:, t, cols], st(RSTD + t), fw[:, cols],
                                                   ALU.mult, ALU.mult).then_inc(fin_ready, 1)

        @block.gpsimd
        def _(pool):
            tt = nc.gpsimd.tensor_tensor

            def stage_taps(q):
                wait(pool, conv_tap, q * 36)
                nc.gpsimd.tensor_copy(cwc[:, 0:1, :], cw[:, bass.ds(q + 32, 1), :])
                nc.gpsimd.tensor_copy(cwc[:, 1:2, :], cw[:, bass.ds(q + 40, 1), :])
                nc.gpsimd.tensor_copy(cwc[:, 2:6, :], cw[:, bass.ds(q * 4, 4), :]).then_inc(cw_staged, 1)

            def masked_a(q, b):
                t, h0 = b // 2, 4 * (b % 2)
                wait(pool, xp_done, q * 4 + b)
                for i in range(4):
                    d, part = i // 2, i % 2
                    m = tt(va[:, i, :].rearrange("p (h l) -> p h l", h=4),
                           tri[:, LE if d == 0 else GE, :].bitcast(F32).unsqueeze(1).to_broadcast([P, 4, P]),
                           cur[:, (A_LO if part else A_HI) + 2 * t + d, h0:h0 + 4].unsqueeze(2).to_broadcast([P, 4, P]),
                           ALU.mult)
                m.then_inc(va_ready, 1)

            def by_head(ap):
                return ap.rearrange("p (h w) -> p h w", h=GH)

            def heads(col):
                return cur[:, col, :].unsqueeze(2).to_broadcast([P, GH, HP])

            def group(q, last=False):
                wait(pool, y_ready, q * 2)
                nc.gpsimd.tensor_copy(cur[:, :, :].rearrange("p a h -> p (a h)").unsqueeze(1),
                                      par[:, bass.ds(q, 1), :]).then_inc(par_staged, 1)
                pool.wait_ge(par_staged, q + 1)
                masked_a(q, 0)
                masked_a(q, 1)
                masked_a(q, 2)
                masked_a(q, 3)
                for t in (1, 0):
                    pool.wait_ge(xs_evac, q * 2 + t + 1)
                    tt(by_head(xoff[:, t, :]), by_head(xs[:, t, :]), heads(XOFF_SC + t), ALU.mult
                       ).then_inc(xoff_ready, 1)
                if not last:
                    stage_taps(q + 1)
                wait(pool, yt_ready, q * 2)
                wait(pool, ysq_ready, q * 2)
                for t in range(NT):
                    tt(by_head(yb[:, t, :]), by_head(xs[:, t, :]), heads(SKIP), ALU.mult).then_inc(skip_ready, 1)
                y_part(q, 0)
                y_part(q, 1)

            def y_part(q, t):
                pool.wait_ge(skip_ready, q * 2 + t + 1)
                pool.wait_ge(toff_ready, q * 2 + t + 1)
                tt(yb[:, t, :], yb[:, t, :], toff, ALU.add).then_inc(ypart_ready, 1)

            def add_squares(q):
                pool.wait_ge(ysq_ready, q * 2 + 2)
                pool.wait_ge(yss_ready, q + 1)
                tt(st(YSS, 2), st(YSS, 2), st(YCUR, 2), ALU.add).then_inc(yss_ready, 1)

            def keep_h(nb):
                for t in range(NT):
                    pool.wait_ge(o_evac, nb * 2 + t + 1)
                    nc.gpsimd.tensor_copy(h[:, t, bass.ds(nb * NB, NB)], hcur[:, t, :]).then_inc(h_kept, 1)
                pool.wait_ge(hsq_ready, nb * 2 + 2)
                pool.wait_ge(hss_ready, nb + 1)
                tt(st(HSS, 2), st(HSS, 2), st(HCUR, 2), ALU.add).then_inc(hss_ready, 1)

            def mask_bias(q):
                for i in range(AH):
                    pool.wait_ge(bias_full[i % 2], q * 128 + 64 * (i // 2 + 1))
                    v = bias[:, i % 2, :].rearrange("p (t n) -> p t n", t=NT)
                    tt(v, v, win.unsqueeze(1).to_broadcast([P, NT, SEQ]), ALU.add).then_inc(bias_ready, 1)

            nc.gpsimd.memset(st(HSS, 2), 0.0).then_inc(hss_ready, 1)
            pool.wait_ge(cw_ready, 1)
            stage_taps(0)
            pool.wait_ge(tri_ready, 1)
            pool.wait_ge(dt_dve, 3)
            pool.wait_ge(ap_ready, 2)
            pv = par[:, :, :].rearrange("p g (a h) -> p g a h", h=GH)
            for t in range(NT):
                for d in range(2):
                    k = 2 * t + d
                    for col, src in ((A_HI, a_parts[:, 0, t, d * 64:(d + 1) * 64].bitcast(F32)),
                                     (A_LO, a_parts[:, 1, t, d * 64:(d + 1) * 64].bitcast(F32)),
                                     (DT, dtv[:, t * P + d * 64:t * P + (d + 1) * 64])):
                        nc.gpsimd.tensor_copy(pv[:, :, col + k, :], src.rearrange("p (g h) -> p g h", g=GROUPS))
            nc.gpsimd.tensor_copy(pv[:, :, SKIP, :], drow.rearrange("p (g h) -> p g h", g=GROUPS))
            pool.wait_ge(dexp_ready, 1)

            def g8(ap):
                return ap.rearrange("p (g h) -> p g h", g=GROUPS)

            nc.gpsimd.tensor_copy(pv[:, :, Y_SC + 1, :], g8(dexp[:, 0:64]))
            nc.gpsimd.tensor_copy(pv[:, :, Y_SC, :], g8(dexp[:, 128:192]))
            tt(pv[:, :, XOFF_SC, :], g8(dexp[:, 64:128]), g8(dtv[:, 0:64]), ALU.mult)
            tt(pv[:, :, XOFF_SC + 1, :], g8(dexp[:, 192:256]), g8(dtv[:, P + 64:2 * P]), ALU.mult
               ).then_inc(par_ready, 1)
            pool.wait_ge(par_ready, 1)
            group(0)
            with pool.Fori(1, GROUPS - 1) as g:
                add_squares(g - 1)
                group(g)
            add_squares(GROUPS - 2)
            group(GROUPS - 1, last=True)
            add_squares(GROUPS - 1)
            with pool.Fori(0, 4) as nb:
                keep_h(nb)
            pool.wait_ge(win_loaded, 16)
            with pool.Fori(0, GROUPS) as g:
                mask_bias(g)
            pool.wait_ge(ms_ready, 3)
            nc.gpsimd.memset(st(HSS, 2), 0.0).then_inc(hss_ready, 1)
            with pool.Fori(0, 4) as nb:
                pool.wait_ge(fsq_ready, nb * 2 + 2)
                pool.wait_ge(hss_ready, nb + 6)
                tt(st(HSS, 2), st(HSS, 2), st(HCUR, 2), ALU.add).then_inc(hss_ready, 1)


def kernel(**inputs):
    import numpy as _np
    import concourse.bacc as _bacc
    from concourse import mybir as _mybir
    from concourse.bass_utils import run_bass_kernel_spmd as _run

    a = {k: _np.asarray(v) for k, v in inputs.items()}
    i, k = _np.arange(128)[:, None], _np.arange(128)[None, :]
    tri = _np.stack([i <= k, i >= k, i > k, i < k], axis=1).astype(_np.float32).reshape(128, 512)
    c, kc = _np.arange(128)[:, None] % 64, _np.arange(256)[None, :] % 64
    first = _np.clip(c - 8, 0, 48)
    win = _np.where((kc >= first) & (kc < first + 16), 0.0, -1e30).astype(_np.float32)
    cols = _np.clip(_np.arange(64)[None, :] - _np.arange(64)[:, None] + 15, 0, 30)
    rpb_rows = a["na_rpb"][0][:, 4:11][:, :, cols].transpose(0, 2, 1, 3).reshape(32 * 64, 7 * 64)
    conv = _np.concatenate([a["ssm_conv_w"][0], a["ssm_conv_b"]], axis=0)
    arrays = {
        "x": a["x"][0],
        "norm_w": a["norm_w"].reshape(2, 16, 128).transpose(2, 0, 1),
        "final_w": a["final_norm_w"],
        "ssm_w_in": a["ssm_w_in"][0],
        "conv_wb": conv.reshape(8, 48, 128).transpose(2, 1, 0).reshape(128, 48 * 8),
        "dt_bias": a["ssm_dt_bias"].reshape(128),
        "a_log": a["ssm_A_log"].reshape(128),
        "ssm_d": a["ssm_D"].reshape(64),
        "ssm_nw": a["ssm_norm_w"].reshape(32, 128).transpose(1, 0),
        "ssm_w_out": a["ssm_w_out"][0],
        "na_w_in": a["na_w_in"][0],
        "rpb_rows": rpb_rows,
        "na_w_out": a["na_w_out"][0],
        "c_ident": _np.eye(128, dtype=_np.float32),
        "c_tri": tri,
        "c_win": win,
    }
    nc = _bacc.Bacc("TRN2", target_bir_lowering=False, num_devices=1, dynamic_dma_scratch_size=1024)
    feed, args = {}, []
    for name, v in arrays.items():
        v = _np.ascontiguousarray(v)
        feed[f"in_{name}"] = v
        args.append(nc.dram_tensor(f"in_{name}", v.shape, _mybir.dt.from_np(v.dtype), kind="ExternalInput").ap())
    args.append(nc.dram_tensor("out_h", (256, 2048), _mybir.dt.float32, kind="ExternalOutput").ap())
    bidir_hybrid(nc, *args)
    r = _run(nc, [feed], core_ids=[0])
    return r.results[0]["out_h"].reshape(1, 256, 2048)
```

```python
from contextlib import ExitStack

import concourse.bass as bass
from concourse import mybir

F32 = mybir.dt.float32
F32R = mybir.dt.float32r
ACT = mybir.ActivationFunctionType
ALU = mybir.AluOpType

P = 128
SEQ = 256
NT = SEQ // P
DM = 2048
DI = 4096
KM, KI = DM // P, DI // P
GROUPS = 8
GH = 8
HP = 64
TAPS = 7
NB = 512
GRID_W = 64
GRID_H = SEQ // GRID_W
HD = 128
AH = 4
EPS = 1e-5
COL_Z, COL_X, COL_B, COL_C, COL_DT = 0, DI, 2 * DI, 2 * DI + 1024, 2 * DI + 2048

SLAB = 1024
RING = 4
DT_SLABS = 2
SSM, OUT, NA, FIN = 20, 16, 32, 16
SSM0 = DT_SLABS
OUT0 = SSM0 + GROUPS * SSM
NA0 = OUT0 + 4 * OUT
FIN0 = NA0 + GROUPS * NA

A_HI, A_LO, DT, XOFF_SC, Y_SC, SKIP, NPAR = 0, 4, 8, 12, 14, 16, 17
FIN_COLS = [(0, 256), (256, 768), (768, 1280), (1280, 1792), (1792, DM)]
LE, GE, GT, LT = range(4)


def wait(eng, sem, value):
    if isinstance(value, int) and value <= 0:
        return
    eng.wait_ge(sem, value)


def bidir_hybrid(nc, x, norm_w, final_w, ssm_w_in, conv_wb, dt_bias, a_log, ssm_d, ssm_nw, ssm_w_out,
                 na_w_in, rpb_rows, na_w_out, c_ident, c_tri, c_win, out):
    with ExitStack() as ctx:
        def sb(name, shape, dt=F32):
            return ctx.enter_context(nc.sbuf_tensor(name, shape, dt))

        def sem(name):
            return ctx.enter_context(nc.semaphore(name))

        raw = sb("raw", [P, RING, SLAB])
        w_hi = sb("w_hi", [P, RING, SLAB], F32R)
        w_lo = sb("w_lo", [P, RING, SLAB], F32R)
        uT_hi = sb("uT_hi", [P, KM, SEQ], F32R)
        uT_lo = sb("uT_lo", [P, KM, SEQ], F32R)
        yT_hi = sb("yT_hi", [P, KI, SEQ], F32R)
        yT_lo = sb("yT_lo", [P, KI, SEQ], F32R)
        ident = sb("ident", [P, P])
        tri = sb("tri", [P, 4, P], F32R)
        win = sb("win", [P, SEQ])
        nw = sb("nw", [P, 2, KM])
        snw = sb("snw", [P, KI])
        cw = sb("cw", [P, 48, TAPS + 1])
        cwc = sb("cwc", [P, 6, TAPS + 1])
        par = sb("par", [P, GROUPS, NPAR * GH])
        cur = sb("cur", [P, NPAR, GH])
        a_parts = sb("a_parts", [P, 2, NT, 2 * 64], F32R)
        stat = sb("stat", [P, 64])
        front = sb("front", [P, NT * DM])
        h = front[:, :].rearrange("p (t n) -> p t n", t=NT)
        rawbc = front[:, 0:512].rearrange("p (t n) -> p t n", t=NT)
        rawx = front[:, 512:1536].rearrange("p (t n) -> p t n", t=NT)
        cacc = front[:, 1536:3072].rearrange("p (c n) -> p c n", c=6)
        ctanh = front[:, 3072:4096].rearrange("p (c n) -> p c n", c=4)
        va = sb("va", [P, 4, NB], F32R)
        with nc.sbuf_tensor("work", [P, 9984], F32) as work:
            pass
        att = sb("att", [P, 5 * 1024])
        qT_hi, kT_hi, v_hi, v_low = (sb(n, [P, 2, NB], F32R) for n in ("qT_hi", "kT_hi", "v_hi", "v_low"))
        rstd_row = sb("rstd_row", [P, SEQ])
        pT_hi, pT_lo = sb("pT_hi", [P, NB], F32R), sb("pT_lo", [P, NB], F32R)

        def area(at, n, parts=NT):
            return work[:, at:at + n].rearrange("p (t n) -> p t n", t=parts)

        xs, wdt, ztanh, xoff = (area(1024 * i, 1024) for i in range(4))
        gz, yb = area(4096, 1024), area(5120, 1024)
        toff, ebuf = work[:, 6144:6656], work[:, 6656:7168]
        scan = area(7168, 2048, 4)
        cbf, cbb, cbo = area(9216, 256), area(9472, 256), area(9728, 256)
        atanh, _, agz, bias, sc = (att[:, 1024 * i:1024 * (i + 1)].rearrange("p (t n) -> p t n", t=NT)
                                 for i in range(5))
        qT_lo, kT_lo = va[:, 0:2, :], va[:, 2:4, :]
        kT = sc
        gT, o = (att[:, 1024 * i:1024 * (i + 1)].rearrange("p (h n) -> p h n", h=AH) for i in (1, 2))
        hcur, junk = area(8704, 1024), work[:, 7168:7680]
        fw = work[:, 0:DM]
        dtv, dta, dte, brow, arow = (work[:, 256 * i:256 * (i + 1)] for i in range(5))
        dexp = work[:, 1536:1792]
        tri_in = work[:, 2048:2560]
        drow = work[:, 2560:2624]
        dt_turned = work[:, 2624:2880]
        junk2 = area(4096, NT * DM)
        SS, MS, RSTD, RHALF = 0, 2, 4, 6
        YSS, YCUR, YR = 8, 10, 12
        HSS, HCUR, HQ = 14, 16, 18
        MX, NMX, DEN, RDEN = 24, 28, 32, 36
        def st(c, n=1):
            return stat[:, c:c + n]

        bank = [ctx.enter_context(nc.psum_tensor(f"bank{i}", [P, NB], F32)) for i in range(8)]
        TR, XP, YA = bank[5], bank[6], bank[7]

        raw_full = [sem(f"raw_full{i}") for i in range(RING)]
        hi_ready, lo_ready, slab_used = sem("hi_ready"), sem("lo_ready"), sem("slab_used")
        x_loaded = [sem(f"x_loaded{i}") for i in range(4)]
        ident_loaded, nw_loaded, par_loaded = sem("ident_loaded"), sem("nw_loaded"), sem("par_loaded")
        table_ready, dtt_evac, dtt_back = sem("table_ready"), sem("dtt_evac"), sem("dtt_back")
        xt0_ready, u_hi_ready, u_lo_ready = sem("xt0_ready"), sem("u_hi_ready"), sem("u_lo_ready")
        tri_ready, sq_ready, ms_ready, rt_ready, rstd_ready = (
            sem(n) for n in ("tri_ready", "sq_ready", "ms_ready", "rt_ready", "rstd_ready"))
        dt_evac, dt_act, dt_dve, ap_ready, dec_ready, dexp_ready, par_ready = (
            sem(n) for n in ("dt_evac", "dt_act", "dt_dve", "ap_ready", "dec_ready", "dexp_ready", "par_ready"))
        cw_ready, cw_staged, par_staged = sem("cw_ready"), sem("cw_staged"), sem("par_staged")
        bc_evac, x_evac, z_evac = sem("bc_evac"), sem("x_evac"), sem("z_evac")
        bct_ready, xt_ready, xback_ready = sem("bct_ready"), sem("xt_ready"), sem("xback_ready")
        conv_init, conv_tap, ctanh_ready, conv_out = (
            sem(n) for n in ("conv_init", "conv_tap", "ctanh_ready", "conv_out"))
        cb_done, cb_evac, gz_ready, xs_evac = sem("cb_done"), sem("cb_evac"), sem("gz_ready"), sem("xs_evac")
        va_ready, xp_done, e_ready, m_ready = sem("va_ready"), sem("xp_done"), sem("e_ready"), sem("m_ready")
        xoff_ready, skip_ready, wdt_half = sem("xoff_ready"), sem("skip_ready"), sem("wdt_half")
        wdt_ready = sem("wdt_ready")
        yoff_done, toff_ready, ypart_ready, ydiag_done = (
            sem(n) for n in ("yoff_done", "toff_ready", "ypart_ready", "ydiag_done"))
        ysum_ready, y_ready, ysq_ready, yss_ready = (
            sem(n) for n in ("ysum_ready", "y_ready", "ysq_ready", "yss_ready"))
        yt_ready, yt_hi_ready, yt_lo_ready = sem("yt_ready"), sem("yt_hi_ready"), sem("yt_lo_ready")
        yr_ready, x_again, o_first, o_evac, h_kept, hsq_ready, hss_ready, ht_ready, ht_hi, ht_lo = (
            sem(n) for n in ("yr_ready", "x_again", "o_first", "o_evac", "h_kept", "hsq_ready", "hss_ready",
                             "ht_ready", "ht_hi", "ht_lo"))
        v_hi_ready, v_lo = sem("v_hi_ready"), sem("v_lo")
        diag_ready, row_done, row_ready = sem("diag_ready"), sem("row_done"), sem("row_ready")
        g_evac, gt_ready, gt_evac = sem("g_evac"), sem("gt_ready"), sem("gt_evac")
        qt_hi, qt_lo, kt_evac, kt_hi, kt_lo = (sem(n) for n in ("qt_hi", "qt_lo", "kt_evac", "kt_hi", "kt_lo"))
        bias_full = [sem("bias_full0"), sem("bias_full1")]
        bias_ready, s_done, smax, smax_ready, p_ready = (
            sem(n) for n in ("bias_ready", "s_done", "smax", "smax_ready", "p_ready"))
        rden_ready, pn_ready, pt_ready, pt_hi, pt_lo, pv_done, agz_ready = (
            sem(n) for n in ("rden_ready", "pn_ready", "pt_ready", "pt_hi", "pt_lo", "pv_done", "agz_ready"))
        o_ready, ot_hi, ot_lo = sem("o_ready"), sem("ot_hi"), sem("ot_lo")
        f_first, f_evac, fsq_ready, fw_loaded, fin_ready, stored = (
            sem(n) for n in ("f_first", "f_evac", "fsq_ready", "fw_loaded", "fin_ready", "stored"))

        DT_TURN0 = 9

        def slot(j):
            return (DT_SLABS + j) % RING

        def loads(phase, it, j):
            first = 1 if slot(j) < DT_SLABS else 0
            if phase == SSM0:
                return first + 6 * it + 2 + j // RING
            if phase == OUT0:
                return first + 6 * GROUPS + 4 * it + j // RING + 1
            if phase == NA0:
                return first + 6 * GROUPS + 16 + 8 * it + j // RING + 1
            return first + 6 * GROUPS + 16 + 8 * GROUPS + 4 * it + j // RING + 1

        def count(phase, it, j):
            per = {SSM0: SSM, OUT0: OUT, NA0: NA, FIN0: FIN}[phase]
            return phase + per * it + j + 1

        def act_slab(n, s, loaded):
            nc.scalar.wait_ge(raw_full[s], 16 * loaded)
            if not isinstance(n, int) or n > RING:
                nc.scalar.wait_ge(slab_used, n - RING)
            nc.scalar.activation(w_hi[:, s, :], raw[:, s, :], ACT.Copy).then_inc(hi_ready, 1)

        def dve_slab(n, s):
            nc.vector.wait_ge(hi_ready, n)
            nc.vector.tensor_tensor(w_lo[:, s, :], raw[:, s, :], w_hi[:, s, :].bitcast(F32),
                                    ALU.subtract).then_inc(lo_ready, 1)

        def pe_slab(n, s, act_hi, act_lo, kt0, kts, width, outs, first, last, shared=False, tile_free=None,
                    first_done=None):
            pe = nc.tensor
            pe.wait_ge(lo_ready, n)
            for t in range(NT):
                if tile_free is not None:
                    wait(pe, tile_free[0], tile_free[1] + t)
                for k in range(kts):
                    col = slice(k * width, (k + 1) * width)
                    a_h = act_hi[:, kt0 + k, t * P:(t + 1) * P]
                    a_l = act_lo[:, kt0 + k, t * P:(t + 1) * P]
                    opens = first and k == 0 and not (shared and t == 1)
                    closes = last and k == kts - 1
                    pe.matmul(outs[t], a_h, w_hi[:, s, col], start=opens, stop=False, skip_group_check=True)
                    pe.matmul(outs[t], a_h, w_lo[:, s, col], start=False, stop=False, skip_group_check=True)
                    mm = pe.matmul(outs[t], a_l, w_hi[:, s, col], start=False, stop=closes,
                                   skip_group_check=True)
                if t == 0 and first_done is not None:
                    mm.then_inc(first_done, 1)
            mm.then_inc(slab_used, 1)

        def pe_slab_turned(n, s, act_hi, act_lo, kt0, outs, first, last, free=None):
            pe = nc.tensor
            pe.wait_ge(lo_ready, n)
            for b in range(2):
                if free is not None:
                    wait(pe, free[0], free[1] + b)
                for k in range(2):
                    a_h, a_l = act_hi[:, kt0 + k, :], act_lo[:, kt0 + k, :]
                    for i in range(2):
                        at = k * NB + (2 * b + i) * P
                        w_h, w_l = w_hi[:, s, at:at + P], w_lo[:, s, at:at + P]
                        dst = outs[b][:, i * SEQ:(i + 1) * SEQ]
                        pe.matmul(dst, w_h, a_h, start=first and k == 0 and i == 0, stop=False, skip_group_check=True)
                        pe.matmul(dst, w_l, a_h, start=False, stop=False, skip_group_check=True)
                        mm = pe.matmul(dst, w_h, a_l, start=False, stop=last and k == 1, skip_group_check=True)
            mm.then_inc(slab_used, 1)

        w1 = ssm_w_in.rearrange("(k p) n -> p k n", p=P)
        w2 = ssm_w_out.rearrange("(k p) n -> p k n", p=P)
        w3 = na_w_in.rearrange("(k p) n -> p k n", p=P)
        w4 = na_w_out.rearrange("(k p) n -> p k n", p=P)
        x_v = x.rearrange("(t p) n -> p t n", p=P)
        out_v = out.rearrange("(t p) n -> p t n", p=P)

        block = ctx.enter_context(nc.Block())

        @block.sync
        def _(sp):
            def free(n):
                if not isinstance(n, int) or n > RING:
                    sp.wait_ge(lo_ready, n - RING)

            def load(n, s, src, k0, kts, cols, waits_for=1):
                if waits_for:
                    free(n + waits_for - 1)
                sp.dma_start(raw[:, s, :].rearrange("p (k n) -> p k n", k=kts),
                             src[:, k0:k0 + kts, cols]).then_inc(raw_full[s], 16)

            def parameters():
                for dst, src in ((tri_in, c_tri), (win[:, :], c_win), (snw[:, :], ssm_nw),
                                 (cw[:, :, :].rearrange("p c k -> p (c k)"), conv_wb),
                                 (brow[:, 0:P], dt_bias.partition_broadcast(P)),
                                 (arow[:, 0:P], a_log.partition_broadcast(P)),
                                 (drow, ssm_d.partition_broadcast(P))):
                    sp.dma_start(dst, src).then_inc(par_loaded, 16)

            def ssm_slabs(it):
                for j in range(SSM):
                    n, s = count(SSM0, it, j), slot(j)
                    if j == RING - DT_SLABS and isinstance(it, int):
                        parameters()
                    if j < 4:
                        free(n)
                        for half, col in enumerate((COL_B, COL_C)):
                            sp.dma_start(
                                raw[:, s, :].rearrange("p (k h n) -> p k h n", k=4, h=2)[:, :, half, :],
                                w1[:, 4 * j:4 * j + 4, bass.ds(it * P + col, P)]).then_inc(raw_full[s], 16)
                    elif j < 12:
                        load(n, s, w1, 2 * (j - 4), 2, bass.ds(it * NB + COL_X, NB), 2 if j == 11 else 1)
                    else:
                        load(n, s, w1, 2 * (j - 12), 2, bass.ds(it * NB + COL_Z, NB), 0 if j == 12 else 1)

            def load_bias(c, hh):
                k = AH * c + hh
                row = k * GRID_W if isinstance(k, int) else sp.snap(k * GRID_W)
                if not isinstance(k, int) or k >= 2:
                    sp.wait_ge(smax_ready, k - 1)
                for r in range(GRID_H):
                    t, half = r // 2, r % 2
                    sp.dma_start(bias[half * GRID_W:(half + 1) * GRID_W, hh % 2, t * SEQ:(t + 1) * SEQ],
                                 rpb_rows[bass.ds(row, GRID_W), (3 - r) * GRID_W:(7 - r) * GRID_W]
                                 ).then_inc(bias_full[hh % 2], 16)

            def na_slabs(it, prev):
                for j in range(NA):
                    load(count(NA0, it, j), slot(j), w3, 2 * (j % 8), 2,
                         bass.ds(it * NB + (j // 8) * DI, NB))
                    if j in (24, 27):
                        load_bias(it, (j - 24) // 3)
                    if j in (0, 3) and prev is not None:
                        load_bias(prev, 2 + j // 3)

            sp.dma_start(ident[:, :], c_ident).then_inc(ident_loaded, 16)
            for i in range(4):
                cols = slice(i * NB, (i + 1) * NB)
                sp.dma_start(h[:, :, cols], x_v[:, :, cols]).then_inc(x_loaded[i], 16)
                if i == 0:
                    sp.dma_start(nw[:, :, :], norm_w).then_inc(nw_loaded, 16)
            for j in range(DT_SLABS):
                sp.dma_start(raw[:, j, :].rearrange("p (k n) -> p k n", k=8),
                             w1[:, 8 * j:8 * j + 8, COL_DT:COL_DT + P]).then_inc(raw_full[j], 16)
            ssm_slabs(0)
            with sp.Fori(1, GROUPS) as g:
                ssm_slabs(g)
            for j in range(OUT):
                load(count(OUT0, 0, j), slot(j), w2, 2 * j, 2, slice(0, NB))
                if j == 10:
                    sp.wait_ge(xback_ready, 2 * GROUPS)
                    for t in range(NT):
                        sp.dma_start(h[:, t, :], x_v[:, t, :]).then_inc(x_again, 16)
            with sp.Fori(1, 4) as nb:
                for j in range(OUT):
                    load(count(OUT0, nb, j), slot(j), w2, 2 * j, 2, bass.ds(nb * NB, NB))
            na_slabs(0, None)
            with sp.Fori(1, GROUPS) as g:
                na_slabs(g, g - 1)
            for j in range(FIN):
                load(count(FIN0, 0, j), slot(j), w4, 2 * j, 2, slice(0, NB))
                if j in (0, 3):
                    load_bias(GROUPS - 1, 2 + j // 3)
            sp.wait_ge(o_ready, AH * GROUPS)
            sp.dma_start(fw, final_w.partition_broadcast(P)).then_inc(fw_loaded, 16)
            with sp.Fori(1, 4) as nb:
                for j in range(FIN):
                    load(count(FIN0, nb, j), slot(j), w4, 2 * j, 2, bass.ds(nb * NB, NB))
            for i, (c0, c1) in enumerate(FIN_COLS):
                for t in range(NT):
                    sp.wait_ge(fin_ready, NT * i + t + 1)
                    sp.dma_start(out_v[:, t, c0:c1], h[:, t, c0:c1]).then_inc(stored, 16)
            sp.wait_ge(stored, 16 * NT * len(FIN_COLS))

        @block.tensor
        def _(pe):
            def transpose(dst, src):
                return pe.transpose(dst, src, ident[:, :])

            def ssm_slab(it, j):
                n, s = count(SSM0, it, j), slot(j)
                if j < 4:
                    if j == 0:
                        if not isinstance(it, int):
                            pe.wait_ge(bc_evac, it)
                    pe_slab(n, s, uT_hi, uT_lo, 4 * j, 4, 2 * P,
                            [bank[0][:, t * 2 * P:(t + 1) * 2 * P] for t in range(NT)], j == 0, j == 3,
                            shared=True)
                elif j < 12:
                    if j == 4:
                        wait(pe, x_evac, it)
                    pe_slab(n, s, uT_hi, uT_lo, 2 * (j - 4), 2, NB, [bank[1][:, :], bank[2][:, :]],
                            j == 4, j == 11)
                else:
                    if j == 12:
                        wait(pe, z_evac, it)
                    pe_slab(n, s, uT_hi, uT_lo, 2 * (j - 12), 2, NB, [bank[3][:, :], bank[4][:, :]],
                            j == 12, j == 19)

            def x_turn(q, r):
                for i in range(2):
                    for t in range(NT):
                        c = 2 * r + i
                        m = transpose((TR, YA)[r][:, i * SEQ + t * P:i * SEQ + (t + 1) * P],
                                      rawx[:, t, c * P:(c + 1) * P])
                m.then_inc(xt_ready, 1)

            def exponents(q, b):
                pe.wait_ge(va_ready, q * 4 + b + 1)
                if b > 0:
                    pe.wait_ge(e_ready, q * 4 + b)
                for i in range(4):
                    m = pe.matmul(XP[:, :], tri[:, GT if i < 2 else LT, :], va[:, i, :], start=(i == 0), stop=(i == 3))
                m.then_inc(xp_done, 1)

            def y_off(q, t):
                pe.wait_ge(xoff_ready, q * 2 + NT - t)
                if t == 0:
                    pe.wait_ge(e_ready, q * 4 + 4)
                else:
                    pe.wait_ge(toff_ready, q * 2 + 1)
                pe.matmul(XP[:, :], cbo[:, 1 - t, :], xoff[:, 1 - t, :], start=True, stop=True).then_inc(yoff_done, 1)

            def y_diag(q, t):
                pe.wait_ge(m_ready, q * 4 + 2 * t + 2)
                if t == 0:
                    pe.wait_ge(xs_evac, q * 2 + 2)
                else:
                    pe.wait_ge(ysum_ready, q * 2 + 1)
                for i in range(GH):
                    cols = slice(i * HP, (i + 1) * HP)
                    m = pe.matmul(YA[:, cols], scan[:, 2 * t + i // 4, (i % 4) * P:(i % 4 + 1) * P], xs[:, t, cols],
                                  start=True, stop=True)
                m.then_inc(ydiag_done, 1)

            def ssm_step(j, q):
                if j == 5:
                    pe.wait_ge(bc_evac, q + 1)
                    wait(pe, xs_evac, q * 2)
                    for c in range(2):
                        for t in range(NT):
                            m = transpose(TR[:, c * SEQ + t * P:c * SEQ + (t + 1) * P], rawbc[:, t, c * P:(c + 1) * P])
                    m.then_inc(bct_ready, 1)
                if j == 10:
                    pe.wait_ge(conv_out, q * 3 + 1)
                    for t in range(NT):
                        m = pe.matmul(TR[:, t * SEQ:(t + 1) * SEQ], cacc[:, 0, t * P:(t + 1) * P], cacc[:, 1, :],
                                      start=True, stop=True)
                    m.then_inc(cb_done, 1)
                if j == 13:
                    pe.wait_ge(x_evac, q + 1)
                    pe.wait_ge(cb_evac, q + 1)
                    wait(pe, yt_lo_ready, q * 4)
                    x_turn(q, 0)
                    x_turn(q, 1)
                if j == 15:
                    exponents(q, 0)
                if j == 17:
                    exponents(q, 1)
                if j == 19:
                    exponents(q, 2)
                if j == 21:
                    pe.wait_ge(conv_out, q * 3 + 3)
                    for t in range(NT):
                        for c in range(4):
                            m = transpose((TR, YA)[t][:, c * P:(c + 1) * P], cacc[:, 2 + c, t * P:(t + 1) * P])
                        m.then_inc(xback_ready, 1)
                if j == 22:
                    exponents(q, 3)
                if j == 23:
                    y_diag(q, 0)
                if j == 24:
                    y_off(q, 0)
                if j == 26:
                    y_off(q, 1)
                if j == 27:
                    y_diag(q, 1)
                if j == 30:
                    pe.wait_ge(y_ready, q * 2 + 2)
                    for c in range(4):
                        for t in range(NT):
                            at = (c % 2) * SEQ + t * P
                            m = transpose((YA, XP)[c // 2][:, at:at + P], yb[:, t, c * P:(c + 1) * P])
                        if c % 2:
                            m.then_inc(yt_ready, 1)

            def out_slab(nb, j):
                free = None
                if j == 0:
                    if isinstance(nb, int):
                        pe.wait_ge(x_evac, GROUPS)
                    else:
                        free = (o_evac, nb * 2 - 1)
                if isinstance(nb, int):
                    pe.wait_ge(yt_lo_ready, 2 * j + 2)
                pe_slab(count(OUT0, nb, j), slot(j), yT_hi, yT_lo, 2 * j, 2, NB, [bank[1][:, :], bank[2][:, :]],
                        j == 0, j == OUT - 1, tile_free=free, first_done=o_first if j == OUT - 1 else None)

            def out_step(j, nb):
                if j == 17:
                    pe.wait_ge(o_evac, nb * 2 + 2)
                    for c in range(4):
                        for t in range(NT):
                            at = (c % 2) * SEQ + t * P
                            m = transpose((TR, XP)[c // 2][:, at:at + P], hcur[:, t, c * P:(c + 1) * P])
                        if c % 2:
                            m.then_inc(ht_ready, 1)

            def na_slab(it, j):
                b = j // 8
                first = isinstance(it, int)
                free = None
                if j == 0:
                    if first:
                        free = (o_evac, 7)
                    else:
                        pe.wait_ge(v_lo, it * 2)
                if j == 8:
                    pe.wait_ge(z_evac, GROUPS) if first else pe.wait_ge(gt_evac, it * 2)
                if j == 16:
                    pe.wait_ge(qt_lo, it * 2 + 2)
                if j == 24:
                    pe.wait_ge(kt_evac, it * 2 + 2)
                if first and b == 0:
                    pe.wait_ge(ht_lo, 2 * j + 2)
                n, outs = count(NA0, it, j), [bank[1 + 2 * (b % 2)][:, :], bank[2 + 2 * (b % 2)][:, :]]
                if b < 2:
                    pe_slab_turned(n, slot(j), uT_hi, uT_lo, 2 * (j % 8), outs, j % 8 == 0, j % 8 == 7, free=free)
                else:
                    pe_slab(n, slot(j), uT_hi, uT_lo, 2 * (j % 8), 2, NB, outs, j % 8 == 0, j % 8 == 7)

            def head_turn(src, banks, done):
                for i in range(AH):
                    for t in range(NT):
                        at = (i % 2) * SEQ + t * P
                        m = transpose(banks[i // 2][:, at:at + P], src[:, t, i * HD:(i + 1) * HD])
                    if i % 2:
                        m.then_inc(done, 1)

            def na_step(j, q):
                if j == 35:
                    pe.wait_ge(agz_ready, q * 2 + 2)
                    head_turn(agz, (bank[3], bank[4]), gt_ready)
                for i in range(AH):
                    k = q * AH + i
                    if j == 24 + 3 * i:
                        pe.wait_ge(qt_lo, q * 2 + 2)
                        pe.wait_ge(kt_lo, q * 2 + 2)
                        if i > 0:
                            pe.wait_ge(smax, k * 2)
                        for t in range(NT):
                            at = (i % 2) * SEQ
                            q_t, k_t = slice(at + t * P, at + (t + 1) * P), slice(at, at + SEQ)
                            dst = bank[0][:, t * SEQ:(t + 1) * SEQ]
                            pe.matmul(dst, qT_hi[:, i // 2, q_t], kT_hi[:, i // 2, k_t], start=True, stop=False)
                            pe.matmul(dst, qT_hi[:, i // 2, q_t], kT_lo[:, i // 2, k_t], start=False, stop=False)
                            m = pe.matmul(dst, qT_lo[:, i // 2, q_t], kT_hi[:, i // 2, k_t], start=False, stop=True)
                        m.then_inc(s_done, 1)
                    if j == 28 + 3 * i:
                        pe.wait_ge(pn_ready, k + 1)
                        if i > 0:
                            pe.wait_ge(pt_lo, k)
                        for kk in range(NT):
                            for t in range(NT):
                                m = transpose(TR[:, kk * SEQ + t * P:kk * SEQ + (t + 1) * P],
                                              sc[:, i % 2, t * SEQ + kk * P:t * SEQ + (kk + 1) * P])
                        m.then_inc(pt_ready, 1)
                    if j == (31, 34, 38, 40)[i]:
                        pe.wait_ge(pt_lo, k + 1)
                        if i == 0:
                            pe.wait_ge(v_lo, q * 2 + 2)
                        if i > 1:
                            pe.wait_ge(o_ready, k - 1)
                        dst = (XP, YA)[i % 2][:, 0:SEQ]
                        for kk in range(NT):
                            v_d, p_q = slice(i * HD, (i + 1) * HD), slice(kk * SEQ, (kk + 1) * SEQ)
                            pe.matmul(dst, v_hi[:, kk, v_d], pT_hi[:, p_q], start=(kk == 0), stop=False)
                            pe.matmul(dst, v_hi[:, kk, v_d], pT_lo[:, p_q], start=False, stop=False)
                            m = pe.matmul(dst, v_low[:, kk, v_d], pT_hi[:, p_q], start=False, stop=(kk == NT - 1))
                        m.then_inc(pv_done, 1)

            def fin_slab(nb, j):
                free = None
                if j == 0:
                    if isinstance(nb, int):
                        pe.wait_ge(v_lo, 2 * GROUPS)
                    else:
                        free = (f_evac, nb * 2 - 1)
                if isinstance(nb, int):
                    pe.wait_ge(ot_lo, 2 * j + 2)
                pe_slab(count(FIN0, nb, j), slot(j), yT_hi, yT_lo, 2 * j, 2, NB, [bank[1][:, :], bank[2][:, :]],
                        j == 0, j == FIN - 1, tile_free=free, first_done=f_first if j == FIN - 1 else None)

            pe.wait_ge(ident_loaded, 16)
            for c in range(KM):
                if c % 4 == 0:
                    pe.wait_ge(x_loaded[c // 4], 16)
                for t in range(NT):
                    at = (c % 2) * SEQ + t * P
                    m = transpose(bank[c // 2][:, at:at + P], h[:, t, c * P:(c + 1) * P])
                if c % 2:
                    m.then_inc(xt0_ready, 1)
            for j in range(DT_SLABS):
                pe.wait_ge(lo_ready, j + 1)
                for k in range(8):
                    kt, dtt, w = 8 * j + k, bank[1][:, 0:SEQ], slice(k * P, (k + 1) * P)
                    pe.wait_ge(u_lo_ready, max(kt + 1, 4))
                    pe.matmul(dtt, w_hi[:, j, w], uT_hi[:, kt, :], start=(kt == 0), stop=False,
                              skip_group_check=True)
                    pe.matmul(dtt, w_lo[:, j, w], uT_hi[:, kt, :], start=False, stop=False,
                              skip_group_check=True)
                    m = pe.matmul(dtt, w_hi[:, j, w], uT_lo[:, kt, :], start=False, stop=(kt == KM - 1),
                                  skip_group_check=True)
                m.then_inc(slab_used, 1)
            for j in range(SSM):
                ssm_slab(0, j)
                if j == 1:
                    pe.wait_ge(dtt_evac, 1)
                    for t in range(NT):
                        m = transpose(XP[:, t * P:(t + 1) * P], dt_turned[:, t * P:(t + 1) * P])
                    m.then_inc(dtt_back, 1)
                if j == 6:
                    pe.wait_ge(ap_ready, 2)
                    for i, (m_, t, d) in enumerate(((LE, 1, 0), (GT, 0, 0), (GE, 0, 1), (LT, 1, 1))):
                        for part in range(2):
                            m = pe.matmul(XP[:, i * 64:(i + 1) * 64], tri[:, m_, :],
                                          a_parts[:, part, t, d * 64:(d + 1) * 64], start=(part == 0), stop=(part == 1))
                    m.then_inc(dec_ready, 1)
                ssm_step(j, 0)
            with pe.Fori(1, GROUPS) as g:
                for j in range(SSM):
                    ssm_slab(g, j)
                    ssm_step(SSM + j, g - 1)
                    ssm_step(j, g)
            for j in range(OUT):
                out_slab(0, j)
                ssm_step(SSM + j, GROUPS - 1)
            with pe.Fori(1, 4) as nb:
                for j in range(OUT):
                    out_slab(nb, j)
                    out_step(OUT + j, nb - 1)
            for j in range(NA):
                na_slab(0, j)
                out_step(OUT + j, 3)
                if j == 9:
                    pe.wait_ge(diag_ready, 1)
                    for i, m_ in enumerate((LE, GT)):
                        m = pe.matmul(XP[:, 0:SEQ], tri[:, m_, :].bitcast(F32), kT[:, 0, 0:SEQ],
                                      start=(i == 0), stop=(i == 1))
                    m.then_inc(row_done, 1)
                na_step(j, 0)
            with pe.Fori(1, GROUPS) as g:
                for j in range(NA):
                    na_slab(g, j)
                    na_step(NA + j, g - 1)
                    na_step(j, g)
            for j in range(FIN):
                fin_slab(0, j)
                na_step(NA + j, GROUPS - 1)
            with pe.Fori(1, 4) as nb:
                for j in range(FIN):
                    fin_slab(nb, j)

        @block.scalar
        def _(act):
            def root():
                return nc.scalar.activation(st(MS, 2), st(MS, 2), ACT.Sqrt)

            def conv_start(q, banks, first, which):
                for i in range(2):
                    m = nc.scalar.activation(cacc[:, first + i, :], banks[:, i * SEQ:(i + 1) * SEQ], ACT.Identity,
                                             scale=cwc[:, first + i, 3:4], bias=cwc[:, first + i, TAPS:TAPS + 1])
                m.then_inc(conv_init, 1)

            def conv_tanh(q, first, at, which):
                act.wait_ge(conv_tap, q * 36 + 12 * (which + 1))
                if which != 1:
                    wait(act, conv_out, q * 3 + which)
                nc.scalar.activation(ctanh[:, at:at + 2, :], cacc[:, first:first + 2, :], ACT.Tanh
                                     ).then_inc(ctanh_ready, 1)

            def ssm_step(j, q):
                if j == 7:
                    act.wait_ge(slab_used, count(SSM0, q, 3))
                    for t in range(NT):
                        m = nc.scalar.activation(rawbc[:, t, :], bank[0][:, t * 2 * P:(t + 1) * 2 * P], ACT.Copy,
                                                 scale=st(RSTD + t))
                    m.then_inc(bc_evac, 1)
                if j == 9:
                    act.wait_ge(bct_ready, q + 1)
                    act.wait_ge(cw_staged, q + 1)
                    conv_start(q, TR, 0, 0)
                if j == 11:
                    conv_tanh(q, 0, 0, 0)
                if j == 15:
                    act.wait_ge(slab_used, count(SSM0, q, 11))
                    for t in range(NT):
                        m = nc.scalar.activation(rawx[:, t, :], bank[1 + t][:, :], ACT.Copy, scale=st(RSTD + t))
                    m.then_inc(x_evac, 1)
                if j == 17:
                    wait(act, xback_ready, q * 2)
                    act.wait_ge(xt_ready, q * 2 + 1)
                    conv_start(q, TR, 2, 1)
                    act.wait_ge(xt_ready, q * 2 + 2)
                    conv_start(q, YA, 4, 2)
                if j == 19:
                    exp_x(q, 0)
                if j == 20:
                    conv_tanh(q, 2, 2, 1)
                if j == 21:
                    exp_x(q, 1)
                if j == 22:
                    conv_tanh(q, 4, 0, 2)
                if j == 23:
                    exp_x(q, 2)
                    act.wait_ge(slab_used, count(SSM0, q, 19))
                    for t in range(NT):
                        nc.scalar.activation(gz[:, t, :], bank[3 + t][:, :], ACT.Copy, scale=st(RHALF + t))
                        m = nc.scalar.activation(ztanh[:, t, :], bank[3 + t][:, :], ACT.Tanh, scale=st(RHALF + t))
                    m.then_inc(z_evac, 1)
                if j == 24:
                    for t in range(NT):
                        act.wait_ge(xback_ready, q * 2 + t + 1)
                        nc.scalar.activation(xs[:, t, :], (TR, YA)[t][:, :], ACT.Copy).then_inc(xs_evac, 1)
                if j == 26:
                    exp_x(q, 3)
                if j == 33:
                    for t in range(NT):
                        act.wait_ge(y_ready, q * 2 + t + 1)
                        act.wait_ge(m_ready, q * 4 + 4)
                        if t:
                            act.wait_ge(ysq_ready, q * 2 + t)
                        nc.scalar.activation(ebuf, yb[:, t, :], ACT.Square, accum_out=st(YCUR + t)
                                             ).then_inc(ysq_ready, 1)
                    for c in range(4):
                        act.wait_ge(yt_ready, q * 2 + c // 2 + 1)
                        nc.scalar.activation(yT_hi[:, bass.ds(q * 4 + c, 1), :], (YA, XP)[c // 2][:, (c % 2) * SEQ:
                                             (c % 2 + 1) * SEQ].unsqueeze(1), ACT.Copy,
                                             scale=snw[:, bass.ds(q * 4 + c, 1)]).then_inc(yt_hi_ready, 1)

            def exp_x(q, b):
                act.wait_ge(xp_done, q * 4 + b + 1)
                if b == 0:
                    wait(act, ysq_ready, q * 2)
                wait(act, m_ready, q * 4 + b)
                nc.scalar.activation(ebuf, XP[:, :], ACT.Exp).then_inc(e_ready, 1)

            def out_step(j, nb):
                if j == 19:
                    for t in range(NT):
                        act.wait_ge(o_evac, nb * 2 + t + 1)
                        act.wait_ge(hss_ready, nb + 1)
                        if t:
                            act.wait_ge(hsq_ready, nb * 2 + t)
                        nc.scalar.activation(junk, hcur[:, t, :], ACT.Square, accum_out=st(HCUR + t)
                                             ).then_inc(hsq_ready, 1)
                if j == 20:
                    for c in range(4):
                        act.wait_ge(ht_ready, nb * 2 + c // 2 + 1)
                        nc.scalar.activation(uT_hi[:, bass.ds(nb * 4 + c, 1), :], (TR, XP)[c // 2][:, (c % 2) * SEQ:
                                             (c % 2 + 1) * SEQ].unsqueeze(1), ACT.Copy,
                                             scale=nw[:, 1, bass.ds(nb * 4 + c, 1)]).then_inc(ht_hi, 1)

            def na_step(j, q):
                if j == 12:
                    wait(act, s_done, q * 4)
                    act.wait_ge(slab_used, count(NA0, q, 7))
                    for i in range(2):
                        nc.scalar.activation(qT_hi[:, i, :], bank[1 + i][:, :], ACT.Copy).then_inc(qt_hi, 1)
                if j == 21:
                    for i in range(2):
                        act.wait_ge(kt_evac, q * 2 + i + 1)
                        nc.scalar.activation(kT_hi[:, i, :], kT[:, i, :], ACT.Copy).then_inc(kt_hi, 1)
                if j == 27:
                    wait(act, pv_done, q * AH)
                    act.wait_ge(slab_used, count(NA0, q, 23))
                    for t in range(NT):
                        nc.scalar.activation(v_hi[:, t, :], bank[1 + t][:, :], ACT.Copy, scale=st(RSTD + t)
                                             ).then_inc(v_hi_ready, 1)
                if j == 35:
                    act.wait_ge(slab_used, count(NA0, q, 31))
                    for t in range(NT):
                        nc.scalar.activation(agz[:, t, :], bank[3 + t][:, :], ACT.Copy, scale=st(RHALF + t))
                        m = nc.scalar.activation(atanh[:, t, :], bank[3 + t][:, :], ACT.Tanh, scale=st(RHALF + t))
                    m.then_inc(g_evac, 1)
                if j == 39:
                    for i in range(2):
                        act.wait_ge(gt_ready, q * 2 + i + 1)
                        nc.scalar.activation(gT[:, 2 * i:2 * i + 2, :], bank[3 + i][:, :], ACT.Copy
                                             ).then_inc(gt_evac, 1)
                for i in range(AH):
                    k = q * AH + i
                    if j == 29 + 3 * i:
                        act.wait_ge(smax_ready, k + 1)
                        for t in range(NT):
                            m = nc.scalar.activation(sc[:, i % 2, t * SEQ:(t + 1) * SEQ],
                                                     sc[:, i % 2, t * SEQ:(t + 1) * SEQ], ACT.Exp,
                                                     bias=st(NMX + 2 * (i % 2) + t),
                                                     accum_out=st(DEN + 2 * (i % 2) + t))
                        m.then_inc(p_ready, 1)
                    if j == 32 + 3 * i:
                        act.wait_ge(pt_ready, k + 1)
                        if i > 0:
                            act.wait_ge(pv_done, k)
                        nc.scalar.activation(pT_hi[:, :], TR[:, :], ACT.Copy).then_inc(pt_hi, 1)
                    if j == (41, 42, 43, 45)[i]:
                        act.wait_ge(o_ready, k + 1)
                        nc.scalar.activation(yT_hi[:, bass.ds(k, 1), :], o[:, i:i + 1, :], ACT.Copy
                                             ).then_inc(ot_hi, 1)

            def fin_step(j, nb):
                if j == 18:
                    for t in range(NT):
                        act.wait_ge(f_evac, nb * 2 + t + 1)
                        act.wait_ge(hss_ready, nb + 6)
                        if t:
                            act.wait_ge(fsq_ready, nb * 2 + t)
                        nc.scalar.activation(junk, h[:, t, bass.ds(nb * NB, NB)], ACT.Square,
                                             accum_out=st(HCUR + t)).then_inc(fsq_ready, 1)

            act.wait_ge(hss_ready, 1)
            nc.scalar.activation(st(HCUR), st(HSS), ACT.Copy).then_inc(table_ready, 1)
            act.wait_ge(nw_loaded, 16)
            for c in range(KM):
                act.wait_ge(xt0_ready, c // 2 + 1)
                nc.scalar.activation(uT_hi[:, c, :], bank[c // 2][:, (c % 2) * SEQ:(c % 2 + 1) * SEQ], ACT.Copy,
                                     scale=nw[:, 0, c:c + 1]).then_inc(u_hi_ready, 1)
                if c in (DT_TURN0, 15):
                    act_slab(1 + c // 15, c // 15, 1)
            for j in range(SSM):
                act_slab(count(SSM0, 0, j), slot(j), loads(SSM0, 0, j))
                if j in (1, 2):
                    nc.scalar.activation(junk2[:, j - 1, :], h[:, j - 1, :], ACT.Square, accum_out=st(SS + j - 1)
                                         ).then_inc(sq_ready, 1)
                if j == 3:
                    act.wait_ge(slab_used, DT_SLABS)
                    nc.scalar.activation(dt_turned, bank[1][:, 0:SEQ], ACT.Copy).then_inc(dtt_evac, 1)
                    act.wait_ge(ms_ready, 1)
                    root().then_inc(rt_ready, 1)
                    act.wait_ge(par_loaded, 16 * 7)
                    nc.scalar.activation(arow[:, 0:P], arow[:, 0:P], ACT.Exp).then_inc(dt_act, 1)
                if j == 5:
                    act.wait_ge(dt_evac, NT)
                    nc.scalar.activation(dte, dtv, ACT.Abs).then_inc(dt_act, 1)
                    act.wait_ge(dt_act, 2)
                    nc.scalar.activation(dte, dte, ACT.Exp, scale=-1.0).then_inc(dt_act, 1)
                if j == 6:
                    act.wait_ge(dt_dve, 1)
                    nc.scalar.activation(dte, dte, ACT.Ln).then_inc(dt_act, 1)
                if j == 10:
                    act.wait_ge(dec_ready, 1)
                    nc.scalar.activation(dexp, XP[:, 0:256], ACT.Exp).then_inc(dexp_ready, 1)
                ssm_step(j, 0)
            with act.Fori(1, GROUPS) as g:
                for j in range(SSM):
                    act_slab(count(SSM0, g, j), slot(j), loads(SSM0, g, j))
                    ssm_step(SSM + j, g - 1)
                    ssm_step(j, g)
            for j in range(OUT):
                act_slab(count(OUT0, 0, j), slot(j), loads(OUT0, 0, j))
                ssm_step(SSM + j, GROUPS - 1)
                if j == 15:
                    act.wait_ge(ms_ready, 2)
                    root().then_inc(rt_ready, 1)
            with act.Fori(1, 4) as nb:
                for j in range(OUT):
                    act_slab(count(OUT0, nb, j), slot(j), loads(OUT0, nb, j))
                    out_step(OUT + j, nb - 1)
            for j in range(NA):
                act_slab(count(NA0, 0, j), slot(j), loads(NA0, 0, j))
                out_step(OUT + j, 3)
                if j == 6:
                    act.wait_ge(ms_ready, 3)
                    root().then_inc(rt_ready, 1)
                if j == 11:
                    act.wait_ge(rstd_ready, 3)
                if j == 13:
                    act.wait_ge(row_done, 1)
                    nc.scalar.activation(rstd_row[:, :], XP[:, 0:SEQ], ACT.Copy).then_inc(row_ready, 1)
                na_step(j, 0)
            with act.Fori(1, GROUPS) as g:
                for j in range(NA):
                    act_slab(count(NA0, g, j), slot(j), loads(NA0, g, j))
                    na_step(NA + j, g - 1)
                    na_step(j, g)
            for j in range(FIN):
                act_slab(count(FIN0, 0, j), slot(j), loads(FIN0, 0, j))
                na_step(NA + j, GROUPS - 1)
            with act.Fori(1, 4) as nb:
                for j in range(FIN):
                    act_slab(count(FIN0, nb, j), slot(j), loads(FIN0, nb, j))
                    fin_step(FIN + j, nb - 1)
            act.wait_ge(hss_ready, 9)
            nc.scalar.activation(st(SS), st(HSS), ACT.Sqrt).then_inc(table_ready, 1)
            fin_step(18, 3)
            act.wait_ge(ms_ready, 6)
            root().then_inc(rt_ready, 1)

        @block.vector
        def _(dve):
            tt = nc.vector.tensor_tensor

            def mean_square(ss, n):
                nc.vector.tensor_scalar(st(MS, 2), st(ss, 2), 1.0 / n, EPS, ALU.mult, ALU.add).then_inc(ms_ready, 1)

            def heads(col, n=GH, first=0, width=HP):
                return cur[:, col, first:first + n].unsqueeze(2).to_broadcast([P, n, width])

            def by_head(ap, n=GH):
                return ap.rearrange("p (h w) -> p h w", h=n)

            def taps(q, bank_, first, which, half):
                if half == 0:
                    dve.wait_ge(conv_init, q * 3 + which + 1)
                n = 12 * which + 6 * half
                for k in ((0, 1, 2), (4, 5, 6))[half]:
                    lo, hi = max(0, 3 - k), min(SEQ, SEQ + 3 - k)
                    for i in range(2):
                        if k > 0:
                            dve.wait_ge(conv_tap, q * 36 + n - 1)
                        acc = cacc[:, first + i, lo:hi]
                        src = bank_[:, i * SEQ + lo + k - 3:i * SEQ + hi + k - 3]
                        nc.vector.scalar_tensor_tensor(acc, src, cwc[:, first + i, k:k + 1], acc, ALU.mult, ALU.add
                                                       ).then_inc(conv_tap, 1)
                        n += 1

            def silu(q, first, at, which):
                dve.wait_ge(ctanh_ready, q * 3 + which + 1)
                nc.vector.scalar_tensor_tensor(cacc[:, first:first + 2, :], ctanh[:, at:at + 2, :], 1.0,
                                               cacc[:, first:first + 2, :], ALU.add, ALU.mult).then_inc(conv_out, 1)

            def weights(q, b):
                t = b // 2
                w = wdt[:, b % 2, :]
                for i in range(4):
                    hh = 4 * (b % 2) + i
                    nc.vector.tensor_scalar(w[:, i * P:(i + 1) * P], cbf[:, t, :], cur[:, DT + 2 * t, hh:hh + 1],
                                            None, ALU.mult).then_inc(wdt_half, 1)
                for i in range(4):
                    hh = 4 * (b % 2) + i
                    dve.wait_ge(wdt_half, q * 16 + b * 4 + i + 1)
                    m = nc.vector.scalar_tensor_tensor(w[:, i * P:(i + 1) * P], cbb[:, t, :],
                                                       cur[:, DT + 2 * t + 1, hh:hh + 1], w[:, i * P:(i + 1) * P],
                                                       ALU.mult, ALU.add)
                m.then_inc(wdt_ready, 1)

            def m_products(q, b):
                dve.wait_ge(e_ready, q * 4 + b + 1)
                dve.wait_ge(wdt_ready, q * 4 + b + 1)
                tt(scan[:, b, :], ebuf, wdt[:, b % 2, :], ALU.mult).then_inc(m_ready, 1)

            def y_sum(q, t):
                dve.wait_ge(ydiag_done, q * 2 + t + 1)
                dve.wait_ge(ypart_ready, q * 2 + t + 1)
                tt(yb[:, t, :], YA[:, :], yb[:, t, :], ALU.add).then_inc(ysum_ready, 1)
                dve.wait_ge(ysum_ready, q * 2 + t + 1)
                dve.wait_ge(gz_ready, q + 1)
                tt(yb[:, t, :], yb[:, t, :], gz[:, t, :], ALU.mult).then_inc(y_ready, 1)

            def y_tile_off(q, t):
                dve.wait_ge(yoff_done, q * 2 + t + 1)
                if t == 1:
                    dve.wait_ge(ypart_ready, q * 2 + 1)
                tt(by_head(toff), by_head(XP[:, :]), heads(Y_SC + t), ALU.mult).then_inc(toff_ready, 1)

            def ssm_step(j, q):
                if j in (9, 10):
                    taps(q, TR, 0, 0, j - 9)
                if j == 12:
                    silu(q, 0, 0, 0)
                if j == 14:
                    dve.wait_ge(cb_done, q + 1)
                    wait(dve, yoff_done, q * 2)
                    for t in range(NT):
                        diag = TR[:, t * (SEQ + P):t * (SEQ + P) + P]
                        tt(cbf[:, t, :], diag, tri[:, LE, :].bitcast(F32), ALU.mult)
                        tt(cbb[:, t, :], diag, tri[:, GE, :].bitcast(F32), ALU.mult)
                    nc.vector.tensor_copy(work[:, 9728:9984], TR[:, P:P + SEQ]).then_inc(cb_evac, 1)
                if j == 15:
                    dve.wait_ge(cb_evac, q + 1)
                    dve.wait_ge(par_staged, q + 1)
                    weights(q, 0)
                if j == 16:
                    weights(q, 1)
                if j in (17, 18):
                    taps(q, TR, 2, 1, j - 17)
                if j in (19, 20):
                    taps(q, YA, 4, 2, j - 19)
                if j == 20:
                    m_products(q, 0)
                if j == 21:
                    silu(q, 2, 2, 1)
                if j == 22:
                    m_products(q, 1)
                if j == 23:
                    silu(q, 4, 0, 2)
                if j == 24:
                    weights(q, 2)
                    dve.wait_ge(z_evac, q + 1)
                    nc.vector.scalar_tensor_tensor(gz[:, :, :], ztanh[:, :, :], 1.0, gz[:, :, :], ALU.add, ALU.mult
                                                   ).then_inc(gz_ready, 1)
                if j == 25:
                    m_products(q, 2)
                    weights(q, 3)
                if j == 27:
                    m_products(q, 3)
                    y_tile_off(q, 0)
                if j == 28:
                    y_sum(q, 0)
                if j == 29:
                    y_tile_off(q, 1)
                if j == 31:
                    y_sum(q, 1)
                if j == 33:
                    for c in range(4):
                        dve.wait_ge(yt_hi_ready, q * 4 + c // 2 * 2 + 2)
                        kt = bass.ds(q * 4 + c, 1)
                        nc.vector.scalar_tensor_tensor(yT_lo[:, kt, :], (YA, XP)[c // 2][:, (c % 2) * SEQ:
                                                       (c % 2 + 1) * SEQ].unsqueeze(1), snw[:, kt],
                                                       yT_hi[:, kt, :].bitcast(F32), ALU.mult, ALU.subtract
                                                       ).then_inc(yt_lo_ready, 1)

            def out_step(j, nb):
                if j == 17:
                    for t in range(NT):
                        if t == 0:
                            dve.wait_ge(o_first, nb + 1)
                        else:
                            dve.wait_ge(slab_used, count(OUT0, nb, OUT - 1))
                        dve.wait_ge(hss_ready, nb + 1)
                        nc.vector.scalar_tensor_tensor(hcur[:, t, :], bank[1 + t][:, :], st(YR + t),
                                                       h[:, t, bass.ds(nb * NB, NB)], ALU.mult, ALU.add
                                                       ).then_inc(o_evac, 1)
                if j == 20:
                    for c in range(4):
                        dve.wait_ge(ht_hi, nb * 4 + c // 2 * 2 + 2)
                        kt = bass.ds(nb * 4 + c, 1)
                        nc.vector.scalar_tensor_tensor(uT_lo[:, kt, :], (TR, XP)[c // 2][:, (c % 2) * SEQ:
                                                       (c % 2 + 1) * SEQ].unsqueeze(1), nw[:, 1, kt],
                                                       uT_hi[:, kt, :].bitcast(F32), ALU.mult, ALU.subtract
                                                       ).then_inc(ht_lo, 1)

            def na_step(j, q):
                if j == 13:
                    for i in range(2):
                        dve.wait_ge(qt_hi, q * 2 + i + 1)
                        tt(qT_lo[:, i, :], bank[1 + i][:, :], qT_hi[:, i, :].bitcast(F32), ALU.subtract
                           ).then_inc(qt_lo, 1)
                if j == 20:
                    dve.wait_ge(slab_used, count(NA0, q, 15))
                    wait(dve, pt_ready, q * 4)
                    row = rstd_row[:, :].unsqueeze(1).to_broadcast([P, 2, SEQ])
                    for i in range(2):
                        tt(kT[:, i, :].rearrange("p (h n) -> p h n", h=2),
                           bank[3 + i][:, :].rearrange("p (h n) -> p h n", h=2), row, ALU.mult).then_inc(kt_evac, 1)
                if j == 22:
                    for i in range(2):
                        dve.wait_ge(kt_hi, q * 2 + i + 1)
                        tt(kT_lo[:, i, :], kT[:, i, :], kT_hi[:, i, :].bitcast(F32), ALU.subtract).then_inc(kt_lo, 1)
                if j == 28:
                    for t in range(NT):
                        dve.wait_ge(v_hi_ready, q * 2 + t + 1)
                        nc.vector.scalar_tensor_tensor(v_low[:, t, :], bank[1 + t][:, :], st(RSTD + t),
                                                       v_hi[:, t, :].bitcast(F32), ALU.mult, ALU.subtract
                                                       ).then_inc(v_lo, 1)
                for i in range(AH):
                    k, m = q * AH + i, 2 * (i % 2)
                    s3 = sc[:, i % 2, :].rearrange("p (t n) -> p t n", t=NT)
                    if j == 28 + 3 * i:
                        dve.wait_ge(s_done, k + 1)
                        dve.wait_ge(bias_ready, k + 1)
                        if i > 1:
                            dve.wait_ge(pt_ready, k - 1)
                        for t in range(NT):
                            cols = slice(t * SEQ, (t + 1) * SEQ)
                            d = nc.vector.scalar_tensor_tensor(sc[:, i % 2, cols], bank[0][:, cols], st(HQ + t),
                                                               bias[:, i % 2, cols], ALU.mult, ALU.add)
                        d.then_inc(smax, 1)
                        dve.wait_ge(smax, k * 2 + 1)
                        nc.vector.tensor_reduce(st(MX + m, 2), s3, mybir.AxisListType.X, ALU.max).then_inc(smax, 1)
                        dve.wait_ge(smax, k * 2 + 2)
                        nc.vector.tensor_scalar(st(NMX + m, 2), st(MX + m, 2), -1.0, None, ALU.mult
                                                ).then_inc(smax_ready, 1)
                    if j == 30 + 3 * i:
                        dve.wait_ge(p_ready, k + 1)
                        nc.vector.reciprocal(st(RDEN + m, 2), st(DEN + m, 2)).then_inc(rden_ready, 1)
                        dve.wait_ge(rden_ready, k + 1)
                        tt(s3, s3, st(RDEN + m, 2).unsqueeze(2).to_broadcast([P, NT, SEQ]), ALU.mult
                           ).then_inc(pn_ready, 1)
                    if j == 33 + 3 * i:
                        dve.wait_ge(pt_hi, k + 1)
                        tt(pT_lo[:, :], TR[:, :], pT_hi[:, :].bitcast(F32), ALU.subtract).then_inc(pt_lo, 1)
                    if j == (40, 41, 42, 44)[i]:
                        dve.wait_ge(pv_done, k + 1)
                        dve.wait_ge(gt_evac, q * 2 + i // 2 + 1)
                        tt(o[:, i, :], (XP, YA)[i % 2][:, 0:SEQ], gT[:, i, :], ALU.mult).then_inc(o_ready, 1)
                    if j == (41, 42, 43, 45)[i]:
                        dve.wait_ge(ot_hi, k + 1)
                        tt(yT_lo[:, bass.ds(k, 1), :], o[:, i:i + 1, :], yT_hi[:, bass.ds(k, 1), :].bitcast(F32),
                           ALU.subtract).then_inc(ot_lo, 1)
                if j == 36:
                    dve.wait_ge(g_evac, q + 1)
                    for t in range(NT):
                        nc.vector.scalar_tensor_tensor(agz[:, t, :], atanh[:, t, :], 1.0, agz[:, t, :], ALU.add,
                                                       ALU.mult).then_inc(agz_ready, 1)

            def fin_step(j, nb):
                if j == 17:
                    for t in range(NT):
                        if t == 0:
                            dve.wait_ge(f_first, nb + 1)
                        else:
                            dve.wait_ge(slab_used, count(FIN0, nb, FIN - 1))
                        hn = h[:, t, bass.ds(nb * NB, NB)]
                        tt(hn, bank[1 + t][:, :], hn, ALU.add).then_inc(f_evac, 1)

            for c in range(KM):
                dve.wait_ge(u_hi_ready, c // 2 * 2 + 2)
                nc.vector.scalar_tensor_tensor(uT_lo[:, c, :], bank[c // 2][:, (c % 2) * SEQ:(c % 2 + 1) * SEQ],
                                               nw[:, 0, c:c + 1], uT_hi[:, c, :].bitcast(F32), ALU.mult, ALU.subtract
                                               ).then_inc(u_lo_ready, 1)
                if c in (DT_TURN0, 15):
                    dve_slab(1 + c // 15, c // 15)
            nc.vector.memset(st(YSS, 2), 0.0).then_inc(yss_ready, 1)
            for j in range(SSM):
                dve_slab(count(SSM0, 0, j), slot(j))
                if j == 2:
                    dve.wait_ge(sq_ready, NT)
                    mean_square(SS, DM)
                if j == 3:
                    dve.wait_ge(par_loaded, 16 * 7)
                    nc.vector.tensor_copy(tri[:, :, :].rearrange("p m n -> p (m n)"), tri_in).then_inc(tri_ready, 1)
                    nc.vector.tensor_scalar(cw[:, :, :], cw[:, :, :], 0.5, None, ALU.mult).then_inc(cw_ready, 1)
                    dve.wait_ge(rt_ready, 1)
                    nc.vector.reciprocal(st(RSTD, 2), st(MS, 2)).then_inc(rstd_ready, 1)
                    dve.wait_ge(rstd_ready, 1)
                    nc.vector.tensor_scalar(st(RHALF, 2), st(RSTD, 2), 0.5, None, ALU.mult).then_inc(rstd_ready, 1)
                if j == 4:
                    dve.wait_ge(dtt_back, 1)
                    for t in range(NT):
                        nc.vector.scalar_tensor_tensor(dtv[:, t * P:(t + 1) * P], XP[:, t * P:(t + 1) * P],
                                                       st(RSTD + t), brow[:, 0:P], ALU.mult, ALU.add
                                                       ).then_inc(dt_evac, 1)
                if j == 5:
                    dve.wait_ge(dt_act, 3)
                    nc.vector.tensor_scalar(dte, dte, 1.0, None, ALU.add).then_inc(dt_dve, 1)
                if j == 6:
                    dve.wait_ge(dt_act, 4)
                    nc.vector.scalar_tensor_tensor(dtv, dtv, 0.0, dte, ALU.max, ALU.add).then_inc(dt_dve, 1)
                    dve.wait_ge(dt_dve, 2)
                    v3 = dtv.rearrange("p (t n) -> p t n", t=NT)
                    a3 = dta.rearrange("p (t n) -> p t n", t=NT)
                    nc.vector.scalar_tensor_tensor(a3, v3, -1.0, arow[:, 0:P].unsqueeze(1).to_broadcast([P, NT, P]),
                                                   ALU.mult, ALU.mult).then_inc(dt_dve, 1)
                    dve.wait_ge(dt_dve, 3)
                    nc.vector.tensor_copy(a_parts[:, 0, :, :], a3).then_inc(ap_ready, 1)
                    dve.wait_ge(ap_ready, 1)
                    tt(a_parts[:, 1, :, :], a3, a_parts[:, 0, :, :].bitcast(F32), ALU.subtract).then_inc(ap_ready, 1)
                ssm_step(j, 0)
            with dve.Fori(1, GROUPS) as g:
                for j in range(SSM):
                    dve_slab(count(SSM0, g, j), slot(j))
                    ssm_step(SSM + j, g - 1)
                    ssm_step(j, g)
            for j in range(OUT):
                dve_slab(count(OUT0, 0, j), slot(j))
                ssm_step(SSM + j, GROUPS - 1)
                if j == 15:
                    dve.wait_ge(yss_ready, GROUPS + 1)
                    mean_square(YSS, DI)
            with dve.Fori(1, 4) as nb:
                for j in range(OUT):
                    dve_slab(count(OUT0, nb, j), slot(j))
                    if j == 0:
                        dve.wait_ge(rt_ready, 2)
                        nc.vector.reciprocal(st(YR, 2), st(MS, 2)).then_inc(yr_ready, 1)
                        dve.wait_ge(yr_ready, nb)
                        dve.wait_ge(x_again, 32)
                    out_step(OUT + j, nb - 1)
            for j in range(NA):
                dve_slab(count(NA0, 0, j), slot(j))
                out_step(OUT + j, 3)
                if j == 5:
                    dve.wait_ge(hss_ready, 5)
                    mean_square(HSS, DM)
                if j == 7:
                    dve.wait_ge(rt_ready, 3)
                    nc.vector.reciprocal(st(RSTD, 2), st(MS, 2)).then_inc(yr_ready, 1)
                    dve.wait_ge(yr_ready, 4)
                    nc.vector.tensor_scalar(st(RHALF, 2), st(RSTD, 2), 0.5, None, ALU.mult)
                    nc.vector.tensor_scalar(st(HQ, 2), st(RSTD, 2), float(HD) ** -0.5, None, ALU.mult
                                            ).then_inc(rstd_ready, 1)
                    for t in range(NT):
                        d = nc.vector.tensor_scalar(kT[:, 0, t * P:(t + 1) * P], ident[:, :], st(RSTD + t), None,
                                                    ALU.mult)
                    d.then_inc(diag_ready, 1)
                if j == 20:
                    dve.wait_ge(row_ready, 1)
                na_step(j, 0)
            with dve.Fori(1, GROUPS) as g:
                for j in range(NA):
                    dve_slab(count(NA0, g, j), slot(j))
                    na_step(NA + j, g - 1)
                    na_step(j, g)
            for j in range(FIN):
                dve_slab(count(FIN0, 0, j), slot(j))
                na_step(NA + j, GROUPS - 1)
            with dve.Fori(1, 4) as nb:
                for j in range(FIN):
                    dve_slab(count(FIN0, nb, j), slot(j))
                    fin_step(FIN + j, nb - 1)
            dve.wait_ge(hss_ready, 9)
            mean_square(HSS, DM)
            fin_step(17, 3)
            dve.wait_ge(ms_ready, 4)
            for t in range(NT):
                dve.wait_ge(fsq_ready, 7 + t)
                nc.vector.scalar_tensor_tensor(st(MS + t), st(HCUR + t), 1.0 / DM, st(MS + t), ALU.mult, ALU.add
                                               ).then_inc(ms_ready, 1)
            dve.wait_ge(rt_ready, 4)
            nc.vector.reciprocal(st(RSTD, 2), st(MS, 2)).then_inc(rstd_ready, 1)
            dve.wait_ge(rstd_ready, 4)
            dve.wait_ge(fw_loaded, 16)
            for c0, c1 in FIN_COLS:
                for t in range(NT):
                    cols = slice(c0, c1)
                    nc.vector.scalar_tensor_tensor(h[:, t, cols], h[:, t, cols], st(RSTD + t), fw[:, cols],
                                                   ALU.mult, ALU.mult).then_inc(fin_ready, 1)

        @block.gpsimd
        def _(pool):
            tt = nc.gpsimd.tensor_tensor

            def stage_taps(q):
                wait(pool, conv_tap, q * 36)
                nc.gpsimd.tensor_copy(cwc[:, 0:1, :], cw[:, bass.ds(q + 32, 1), :])
                nc.gpsimd.tensor_copy(cwc[:, 1:2, :], cw[:, bass.ds(q + 40, 1), :])
                nc.gpsimd.tensor_copy(cwc[:, 2:6, :], cw[:, bass.ds(q * 4, 4), :]).then_inc(cw_staged, 1)

            def masked_a(q, b):
                t, h0 = b // 2, 4 * (b % 2)
                wait(pool, xp_done, q * 4 + b)
                for i in range(4):
                    d, part = i // 2, i % 2
                    m = tt(va[:, i, :].rearrange("p (h l) -> p h l", h=4),
                           tri[:, LE if d == 0 else GE, :].bitcast(F32).unsqueeze(1).to_broadcast([P, 4, P]),
                           cur[:, (A_LO if part else A_HI) + 2 * t + d, h0:h0 + 4].unsqueeze(2).to_broadcast([P, 4, P]),
                           ALU.mult)
                m.then_inc(va_ready, 1)

            def by_head(ap):
                return ap.rearrange("p (h w) -> p h w", h=GH)

            def heads(col):
                return cur[:, col, :].unsqueeze(2).to_broadcast([P, GH, HP])

            def group(q, last=False):
                wait(pool, y_ready, q * 2)
                nc.gpsimd.tensor_copy(cur[:, :, :].rearrange("p a h -> p (a h)").unsqueeze(1),
                                      par[:, bass.ds(q, 1), :]).then_inc(par_staged, 1)
                pool.wait_ge(par_staged, q + 1)
                masked_a(q, 0)
                masked_a(q, 1)
                masked_a(q, 2)
                masked_a(q, 3)
                for t in (1, 0):
                    pool.wait_ge(xs_evac, q * 2 + t + 1)
                    tt(by_head(xoff[:, t, :]), by_head(xs[:, t, :]), heads(XOFF_SC + t), ALU.mult
                       ).then_inc(xoff_ready, 1)
                if not last:
                    stage_taps(q + 1)
                wait(pool, yt_ready, q * 2)
                wait(pool, ysq_ready, q * 2)
                for t in range(NT):
                    tt(by_head(yb[:, t, :]), by_head(xs[:, t, :]), heads(SKIP), ALU.mult).then_inc(skip_ready, 1)
                y_part(q, 0)
                y_part(q, 1)

            def y_part(q, t):
                pool.wait_ge(skip_ready, q * 2 + t + 1)
                pool.wait_ge(toff_ready, q * 2 + t + 1)
                tt(yb[:, t, :], yb[:, t, :], toff, ALU.add).then_inc(ypart_ready, 1)

            def add_squares(q):
                pool.wait_ge(ysq_ready, q * 2 + 2)
                pool.wait_ge(yss_ready, q + 1)
                tt(st(YSS, 2), st(YSS, 2), st(YCUR, 2), ALU.add).then_inc(yss_ready, 1)

            def keep_h(nb):
                for t in range(NT):
                    pool.wait_ge(o_evac, nb * 2 + t + 1)
                    nc.gpsimd.tensor_copy(h[:, t, bass.ds(nb * NB, NB)], hcur[:, t, :]).then_inc(h_kept, 1)
                pool.wait_ge(hsq_ready, nb * 2 + 2)
                pool.wait_ge(hss_ready, nb + 1)
                tt(st(HSS, 2), st(HSS, 2), st(HCUR, 2), ALU.add).then_inc(hss_ready, 1)

            def mask_bias(q):
                for i in range(AH):
                    pool.wait_ge(bias_full[i % 2], q * 128 + 64 * (i // 2 + 1))
                    v = bias[:, i % 2, :].rearrange("p (t n) -> p t n", t=NT)
                    tt(v, v, win[:, :].unsqueeze(1).to_broadcast([P, NT, SEQ]), ALU.add).then_inc(bias_ready, 1)

            nc.gpsimd.memset(st(HSS, 2), 0.0).then_inc(hss_ready, 1)
            pool.wait_ge(cw_ready, 1)
            stage_taps(0)
            pool.wait_ge(tri_ready, 1)
            pool.wait_ge(dt_dve, 3)
            pool.wait_ge(ap_ready, 2)
            pv = par[:, :, :].rearrange("p g (a h) -> p g a h", h=GH)
            for t in range(NT):
                for d in range(2):
                    k = 2 * t + d
                    for col, src in ((A_HI, a_parts[:, 0, t, d * 64:(d + 1) * 64].bitcast(F32)),
                                     (A_LO, a_parts[:, 1, t, d * 64:(d + 1) * 64].bitcast(F32)),
                                     (DT, dtv[:, t * P + d * 64:t * P + (d + 1) * 64])):
                        nc.gpsimd.tensor_copy(pv[:, :, col + k, :], src.rearrange("p (g h) -> p g h", g=GROUPS))
            nc.gpsimd.tensor_copy(pv[:, :, SKIP, :], drow.rearrange("p (g h) -> p g h", g=GROUPS))
            pool.wait_ge(dexp_ready, 1)

            def g8(ap):
                return ap.rearrange("p (g h) -> p g h", g=GROUPS)

            nc.gpsimd.tensor_copy(pv[:, :, Y_SC + 1, :], g8(dexp[:, 0:64]))
            nc.gpsimd.tensor_copy(pv[:, :, Y_SC, :], g8(dexp[:, 128:192]))
            tt(pv[:, :, XOFF_SC, :], g8(dexp[:, 64:128]), g8(dtv[:, 0:64]), ALU.mult)
            tt(pv[:, :, XOFF_SC + 1, :], g8(dexp[:, 192:256]), g8(dtv[:, P + 64:2 * P]), ALU.mult
               ).then_inc(par_ready, 1)
            pool.wait_ge(par_ready, 1)
            group(0)
            with pool.Fori(1, GROUPS - 1) as g:
                add_squares(g - 1)
                group(g)
            add_squares(GROUPS - 2)
            group(GROUPS - 1, last=True)
            add_squares(GROUPS - 1)
            with pool.Fori(0, 4) as nb:
                keep_h(nb)
            with pool.Fori(0, GROUPS) as g:
                mask_bias(g)
            pool.wait_ge(ms_ready, 3)
            nc.gpsimd.memset(st(HSS, 2), 0.0).then_inc(hss_ready, 1)
            with pool.Fori(0, 3) as nb:
                pool.wait_ge(fsq_ready, nb * 2 + 2)
                pool.wait_ge(hss_ready, nb + 6)
                tt(st(HSS, 2), st(HSS, 2), st(HCUR, 2), ALU.add).then_inc(hss_ready, 1)


def kernel(**inputs):
    import numpy as _np
    import concourse.bacc as _bacc
    from concourse import mybir as _mybir
    from concourse.bass_utils import run_bass_kernel_spmd as _run

    a = {k: _np.asarray(v) for k, v in inputs.items()}
    i, k = _np.arange(128)[:, None], _np.arange(128)[None, :]
    tri = _np.stack([i <= k, i >= k, i > k, i < k], axis=1).astype(_np.float32).reshape(128, 512)
    c, kc = _np.arange(128)[:, None] % 64, _np.arange(256)[None, :] % 64
    first = _np.clip(c - 8, 0, 48)
    win = _np.where((kc >= first) & (kc < first + 16), 0.0, -1e30).astype(_np.float32)
    cols = _np.clip(_np.arange(64)[None, :] - _np.arange(64)[:, None] + 15, 0, 30)
    rpb_rows = a["na_rpb"][0][:, 4:11][:, :, cols].transpose(0, 2, 1, 3).reshape(32 * 64, 7 * 64)
    conv = _np.concatenate([a["ssm_conv_w"][0], a["ssm_conv_b"]], axis=0)
    arrays = {
        "x": a["x"][0],
        "norm_w": a["norm_w"].reshape(2, 16, 128).transpose(2, 0, 1),
        "final_w": a["final_norm_w"],
        "ssm_w_in": a["ssm_w_in"][0],
        "conv_wb": conv.reshape(8, 48, 128).transpose(2, 1, 0).reshape(128, 48 * 8),
        "dt_bias": a["ssm_dt_bias"].reshape(128),
        "a_log": a["ssm_A_log"].reshape(128),
        "ssm_d": a["ssm_D"].reshape(64),
        "ssm_nw": a["ssm_norm_w"].reshape(32, 128).transpose(1, 0),
        "ssm_w_out": a["ssm_w_out"][0],
        "na_w_in": a["na_w_in"][0],
        "rpb_rows": rpb_rows,
        "na_w_out": a["na_w_out"][0],
        "c_ident": _np.eye(128, dtype=_np.float32),
        "c_tri": tri,
        "c_win": win,
    }
    nc = _bacc.Bacc("TRN2", target_bir_lowering=False, num_devices=1, dynamic_dma_scratch_size=1024)
    feed, args = {}, []
    for name, v in arrays.items():
        v = _np.ascontiguousarray(v)
        feed[f"in_{name}"] = v
        args.append(nc.dram_tensor(f"in_{name}", v.shape, _mybir.dt.from_np(v.dtype), kind="ExternalInput").ap())
    args.append(nc.dram_tensor("out_h", (256, 2048), _mybir.dt.float32, kind="ExternalOutput").ap())
    bidir_hybrid(nc, *args)
    r = _run(nc, [feed], core_ids=[0])
    return r.results[0]["out_h"].reshape(1, 256, 2048)
```
